# Optimizing a Trainium2 kernel written in Bass

```python
import jax, jax.numpy as jnp
from jax import lax
import numpy as np

D_MODEL = 1024
BATCH = 1
SEQ = 512
DEPTH = 2
DEC_BATCH = 8
DEC_SEQ = 1
PAST_LEN = 4096
PAGE_SIZE = 128

CHUNK = 128
A_GROUPS = 4
D_A = D_MODEL // 2
A_GROUP_DIM = D_A // A_GROUPS
D_B = D_MODEL // 2
CONV_B_WIDTH = 3
D_C = D_MODEL // 2
CONV_C_WIDTH = 31
N_BRANCHES = 3
D_BR = D_MODEL // 2
D_IN = 2 * D_A + 3 * D_B + 2 * D_C + N_BRANCHES * D_MODEL
N_KEYS = 128
N_EXPERTS = N_KEYS * N_KEYS
PEER_HEADS = 8
PEER_TOPK = 16
D_KEY = 256
D_KEY_HALF = D_KEY // 2
PEER_BLOCK = 128
EPS = 1e-6

kernel_name = "gated_branch_chunkmlp_shortconv_conformer_peer_decode"

def rmsnorm(x, g):
    xf = x.astype(jnp.float32)
    y = xf * lax.rsqrt(jnp.mean(xf * xf, axis=-1, keepdims=True) + EPS)
    return (y * g.astype(jnp.float32)).astype(x.dtype)

def layernorm(x, g, b):
    xf = x.astype(jnp.float32)
    mu = jnp.mean(xf, axis=-1, keepdims=True)
    var = jnp.mean(jnp.square(xf - mu), axis=-1, keepdims=True)
    y = (xf - mu) * lax.rsqrt(var + EPS)
    return (y * g.astype(jnp.float32) + b.astype(jnp.float32)).astype(x.dtype)

def causal_dwconv(hist, z, w):
    width, ch = w.shape
    zz = jnp.concatenate([hist.astype(z.dtype), z], axis=1)
    y = lax.conv_general_dilated(zz, w[:, None, :].astype(z.dtype), window_strides=(1,), padding='VALID',
                                 dimension_numbers=('NWC', 'WIO', 'NWC'), feature_group_count=ch)
    return y, zz[:, -(width - 1):]

def chunk_spatial_gate(u, v, w_s, b_s):
    bsz, t, _ = v.shape
    pad = (-t) % CHUNK
    vp = jnp.pad(v, ((0, 0), (0, pad), (0, 0)))
    nc = vp.shape[1] // CHUNK
    vc = vp.reshape(bsz, nc, CHUNK, A_GROUPS, A_GROUP_DIM)
    mask = jnp.tril(jnp.ones((CHUNK, CHUNK), dtype=bool))
    w = jnp.where(mask[None], w_s, jnp.zeros_like(w_s)).astype(v.dtype)
    mixed = jnp.einsum('gts,bcsgd->bctgd', w, vc) + jnp.transpose(b_s).astype(v.dtype)[None, None, :, :, None]
    mixed = mixed.reshape(bsz, nc * CHUNK, D_A)[:, :t]
    return u * mixed

def peer(h, w_query, sub_keys, expert_u, expert_v):
    bsz, t, d = h.shape
    xf = h.reshape(bsz * t, d)
    n = xf.shape[0]
    pad = (-n) % PEER_BLOCK
    blocks = jnp.pad(xf, ((0, pad), (0, 0))).reshape(-1, PEER_BLOCK, d)

    def one_block(xb):
        q = (xb @ w_query).reshape(PEER_BLOCK, PEER_HEADS, 2, D_KEY_HALF)
        s = jnp.einsum('thpk,hpnk->thpn', q, sub_keys).astype(jnp.float32)
        s_top, i_top = lax.top_k(s, PEER_TOPK)
        cand = s_top[:, :, 0, :, None] + s_top[:, :, 1, None, :]
        cand_idx = i_top[:, :, 0, :, None] * N_KEYS + i_top[:, :, 1, None, :]
        cand = cand.reshape(PEER_BLOCK, PEER_HEADS, PEER_TOPK * PEER_TOPK)
        cand_idx = cand_idx.reshape(PEER_BLOCK, PEER_HEADS, PEER_TOPK * PEER_TOPK)
        best, pos = lax.top_k(cand, PEER_TOPK)
        idx = jnp.take_along_axis(cand_idx, pos, axis=-1)
        g = jax.nn.softmax(best, axis=-1)
        u = expert_u[idx]
        v = expert_v[idx]
        a = jax.nn.gelu(jnp.einsum('td,thkd->thk', xb, u))
        return jnp.einsum('thk,thkd->td', (g * a.astype(jnp.float32)).astype(v.dtype), v)

    out = lax.map(one_block, blocks).reshape(-1, d)[:n]
    return out.reshape(bsz, t, d).astype(h.dtype)

def trunk_layer(x, c, hist_b, hist_c, norm_g, ada_w, ada_b, w_in, ln_a_g, ln_a_b, w_spatial, b_spatial,
                conv_b_w, conv_c_w, conv_c_b, ln_c_g, ln_c_b, w_branch, w_out,
                peer_w_query, peer_sub_keys, peer_u, peer_v):
    bsz, t, d = x.shape
    mod = (jax.nn.silu(c) @ ada_w + ada_b)[:, None, :]
    shift1, scale1, gate1, shift2, scale2, gate2 = jnp.split(mod, 6, axis=-1)

    h = rmsnorm(x, norm_g[0]) * (1.0 + scale1) + shift1
    z = h @ w_in
    sizes = [D_A, D_A, D_B, D_B, D_B, D_C, D_C]
    cuts = [int(s) for s in np.cumsum(sizes)]
    ua, va, hb, bb, cb, ac, gc, zg = jnp.split(z, cuts, axis=-1)
    ua = jax.nn.gelu(ua)
    va = layernorm(jax.nn.gelu(va), ln_a_g, ln_a_b)
    ya = chunk_spatial_gate(ua, va, w_spatial, b_spatial)
    conv_in_b = cb * hb
    conv_out_b, new_hist_b = causal_dwconv(hist_b, conv_in_b, conv_b_w)
    yb = bb * conv_out_b
    glu = ac * jax.nn.sigmoid(gc)
    conv_out_c, new_hist_c = causal_dwconv(hist_c, glu, conv_c_w)
    yc = jax.nn.silu(layernorm(conv_out_c + conv_c_b, ln_c_g, ln_c_b))
    gates = jax.nn.sigmoid(zg).reshape(bsz, t, N_BRANCHES, d)
    merged = (gates[:, :, 0] * (ya @ w_branch[0]) + gates[:, :, 1] * (yb @ w_branch[1])
              + gates[:, :, 2] * (yc @ w_branch[2]))
    x = x + gate1 * (merged @ w_out)

    h2 = rmsnorm(x, norm_g[1]) * (1.0 + scale2) + shift2
    x = x + gate2 * peer(h2, peer_w_query, peer_sub_keys, peer_u, peer_v)
    return x, va, new_hist_b, new_hist_c

def setup_inputs(seed: int = 0) -> dict:
    key = jax.random.key(seed)
    ks = jax.random.split(key, 30)
    f32 = jnp.float32
    nrm = lambda k, shape, s: jax.random.normal(k, shape, f32) * s
    return {
        "x_prompt": nrm(ks[0], (BATCH, SEQ, D_MODEL), 1.0),
        "x_sample": nrm(ks[1], (DEC_BATCH, DEC_SEQ, D_MODEL), 1.0),
        "c_prompt": nrm(ks[2], (BATCH, D_MODEL), 1.0),
        "c_sample": nrm(ks[3], (DEC_BATCH, D_MODEL), 1.0),
        "state_conv_b": nrm(ks[4], (DEPTH, DEC_BATCH, CONV_B_WIDTH - 1, D_B), 0.5),
        "state_conv_c": nrm(ks[5], (DEPTH, DEC_BATCH, CONV_C_WIDTH - 1, D_C), 0.5),
        "norm_g": 1.0 + nrm(ks[6], (DEPTH, 2, D_MODEL), 0.1),
        "final_g": 1.0 + nrm(ks[7], (D_MODEL,), 0.1),
        "ada_w": nrm(ks[8], (DEPTH, D_MODEL, 6 * D_MODEL), 0.5 * D_MODEL ** -0.5),
        "ada_b": nrm(ks[9], (DEPTH, 6 * D_MODEL), 0.05),
        "w_in": nrm(ks[10], (DEPTH, D_MODEL, D_IN), D_MODEL ** -0.5),
        "ln_a_g": 1.0 + nrm(ks[11], (DEPTH, D_A), 0.1),
        "ln_a_b": nrm(ks[12], (DEPTH, D_A), 0.1),
        "w_spatial": nrm(ks[13], (DEPTH, A_GROUPS, CHUNK, CHUNK), CHUNK ** -0.5),
        "b_spatial": 1.0 + nrm(ks[14], (DEPTH, A_GROUPS, CHUNK), 0.1),
        "conv_b_w": nrm(ks[15], (DEPTH, CONV_B_WIDTH, D_B), CONV_B_WIDTH ** -0.5),
        "conv_c_w": nrm(ks[16], (DEPTH, CONV_C_WIDTH, D_C), CONV_C_WIDTH ** -0.5),
        "conv_c_b": nrm(ks[17], (DEPTH, D_C), 0.1),
        "ln_c_g": 1.0 + nrm(ks[18], (DEPTH, D_C), 0.1),
        "ln_c_b": nrm(ks[19], (DEPTH, D_C), 0.1),
        "w_branch": nrm(ks[20], (DEPTH, N_BRANCHES, D_BR, D_MODEL), D_BR ** -0.5),
        "w_out": nrm(ks[21], (DEPTH, D_MODEL, D_MODEL), D_MODEL ** -0.5),
        "peer_w_query": nrm(ks[22], (DEPTH, D_MODEL, PEER_HEADS * D_KEY), D_MODEL ** -0.5),
        "peer_sub_keys": nrm(ks[23], (DEPTH, PEER_HEADS, 2, N_KEYS, D_KEY_HALF), D_KEY_HALF ** -0.5),
        "peer_u": nrm(ks[24], (DEPTH, N_EXPERTS, D_MODEL), D_MODEL ** -0.5),
        "peer_v": nrm(ks[25], (DEPTH, N_EXPERTS, D_MODEL), PEER_HEADS ** -0.5),
    }

def reference(x_prompt, x_sample, c_prompt, c_sample, state_conv_b, state_conv_c,
              norm_g, final_g, ada_w, ada_b, w_in, ln_a_g, ln_a_b, w_spatial, b_spatial,
              conv_b_w, conv_c_w, conv_c_b, ln_c_g, ln_c_b, w_branch, w_out,
              peer_w_query, peer_sub_keys, peer_u, peer_v):
    bp = x_prompt.shape[0]
    xp, xs = x_prompt, x_sample
    zero_b = jnp.zeros((bp, CONV_B_WIDTH - 1, D_B), x_prompt.dtype)
    zero_c = jnp.zeros((bp, CONV_C_WIDTH - 1, D_C), x_prompt.dtype)
    v_s_list, hb_p_list, hb_s_list, hc_p_list, hc_s_list = [], [], [], [], []
    for l in range(DEPTH):
        lw = (norm_g[l], ada_w[l], ada_b[l], w_in[l], ln_a_g[l], ln_a_b[l], w_spatial[l], b_spatial[l],
              conv_b_w[l], conv_c_w[l], conv_c_b[l], ln_c_g[l], ln_c_b[l], w_branch[l], w_out[l],
              peer_w_query[l], peer_sub_keys[l], peer_u[l], peer_v[l])
        xp, _, hb_p, hc_p = trunk_layer(xp, c_prompt, zero_b, zero_c, *lw)
        xs, v_s, hb_s, hc_s = trunk_layer(xs, c_sample, state_conv_b[l], state_conv_c[l], *lw)
        v_s_list.append(v_s)
        hb_p_list.append(hb_p)
        hb_s_list.append(hb_s)
        hc_p_list.append(hc_p)
        hc_s_list.append(hc_s)
    y_prompt = rmsnorm(xp, final_g)
    y_sample = rmsnorm(xs, final_g)
    new_chunk_v_sample = jnp.stack(v_s_list)
    new_conv_b_prompt = jnp.stack(hb_p_list)
    new_conv_b_sample = jnp.stack(hb_s_list)
    new_conv_c_prompt = jnp.stack(hc_p_list)
    new_conv_c_sample = jnp.stack(hc_s_list)
    return (y_prompt, y_sample, new_chunk_v_sample, new_conv_b_prompt, new_conv_b_sample,
            new_conv_c_prompt, new_conv_c_sample)


_drawn_inputs = setup_inputs


def setup_inputs(seed=0):
    import zlib

    import numpy as np

    out = dict(_drawn_inputs(seed))
    spreads = {}
    factors = {'b_spatial': 2.833, 'ln_c_g': 2.865, 'ln_c_b': 3.403}
    for name, (base, spread) in spreads.items():
        noise = np.random.default_rng([zlib.crc32(name.encode()), seed]).standard_normal(out[name].shape)
        drawn = base * np.exp(spread * noise) if base else spread * noise
        out[name] = __import__('jax').numpy.asarray(drawn.astype(out[name].dtype))
    for name, factor in factors.items():
        out[name] = (out[name] * factor).astype(out[name].dtype)
    return out
```

```python
from contextlib import ExitStack

import concourse.bass as bass
from concourse import mybir

F32 = mybir.dt.float32
F32R = mybir.dt.float32r
U32 = mybir.dt.uint32
ALU = mybir.AluOpType
ACT = mybir.ActivationFunctionType
AX_X = mybir.AxisListType.X

P = 128
D = 1024
KC = D // P
SEQ = 512
NS = 8
T = SEQ + NS
HT = T // 2
H1P = SEQ - HT
NC = 1 + NS
DEPTH = 2
BC = 4
WB, WC = 3, 31
EPS = 1e-6
NMOD = 6 * KC
HEADS, TOPK = 8, 16
HP = 2 * HEADS
NBLK = 128
RT_TOK, RT_N = 104, 5
GB = 40
GBN = T // GB
GS = 10
NEG = -3.0e38

T_V, T_U, T_B, T_C, T_BB, T_BR, T_O, T_Q, T_EU, T_ED = 0, 4, 8, 16, 24, 28, 64, 72, 88, 216
NT = T_ED + NBLK
RAW_PER_SLOT = (NMOD + NT) // 4
M_BR, M_O, M_Q, M_EU, M_ED = 28, 76, 84, 100, 228
NM = M_ED + 8 * 32
G_BR, G_O, G_Q, G_EU, G_ED = 24, 72, 80, 96, 224
NG = (G_ED + 8 * 32) // 2
PAR = {}
_at = 0
for _n, _w in (("ada_b", NMOD), ("norm_g", 2 * KC), ("ln_a_g", 512), ("ln_a_b", 512), ("w_s", 512),
               ("b_s", 512), ("w_s00", BC), ("conv_b", BC * WB), ("conv_c", BC * WC),
               ("conv_c_b", BC), ("ln_c_g", BC), ("ln_c_b", BC)):
    PAR[_n] = (_at, _at + _w)
    _at += _w
NPAR = _at


class Steps:

    def __init__(self, eng, sem):
        self.eng, self.sem, self.n = eng, sem, 0

    def do(self, ins):
        ins.then_inc(self.sem, 1)
        self.n += 1

    def settle(self):
        self.eng.wait_ge(self.sem, self.n)

    def link(self, ins):
        self.do(ins)
        self.settle()

    def restart(self):
        if self.n:
            self.settle()
            self.eng.sem_clear(self.sem)
            self.n = 0


def build(nc, stream, x_t, c_t, final_g, params, hist_b, hist_c, sub_keys,
          y_out, v_out, hb_p, hb_s, hc_p, hc_s):
    hidden_dram = nc.dram_tensor("hidden_dram", (P, NBLK, T), F32).ap()
    gate_dram = nc.dram_tensor("gate_dram", (GBN, P, NBLK, GB), F32).ap()
    stream = stream.rearrange("l n p k m -> (l n) p k m")
    with ExitStack() as ctx:

        def sb(stack, name, shape, dt=F32):
            return stack.enter_context(nc.sbuf_tensor(name, shape, dt))

        def sem(name):
            return ctx.enter_context(nc.semaphore(name))

        raw = sb(ctx, "raw", [P, 4, KC, P])
        w_hi = sb(ctx, "w_hi", [P, 4, KC, P], F32R)
        w_lo = sb(ctx, "w_lo", [P, 4, KC, P], F32R)
        a_hi = sb(ctx, "a_hi", [P, KC * T], F32R)
        a_lo = sb(ctx, "a_lo", [P, KC * T], F32R)
        x = sb(ctx, "x", [P, KC, T])
        par = sb(ctx, "par", [P, NPAR])
        cond = sb(ctx, "cond", [P, KC, NC])
        cond_silu = sb(ctx, "cond_silu", [P, KC, NC])
        mod = sb(ctx, "mod", [P, NMOD, NC])
        mod_scale = sb(ctx, "mod_scale", [P, 2, KC, NC])
        fin_g = sb(ctx, "fin_g", [P, KC])
        ident = sb(ctx, "ident", [P, P])
        ones = sb(ctx, "ones", [P, P])
        iota_u = sb(ctx, "iota_u", [P, P], U32)
        iota_f = sb(ctx, "iota_f", [P, P])
        eps_t = sb(ctx, "eps_t", [P, 1])
        tmp8 = sb(ctx, "tmp8", [P, NS])

        trunk = ExitStack()
        sq = sb(trunk, "sq", [P, 2, T])
        rstd = sb(trunk, "rstd", [P, T])
        nb = sb(trunk, "nb", [P, 2, T])
        merged = sb(trunk, "merged", [P, KC, T])
        glu = sb(trunk, "glu", [P, BC, WC - 1 + SEQ])
        glu_s = sb(trunk, "glu_s", [P, BC, NS, WC])
        ys = sb(trunk, "ys", [P, 3, BC, T])
        pool_tmp = sb(trunk, "pool_tmp", [P, SEQ])
        mix_t = sb(trunk, "mix_t", [P, SEQ])
        v_stat = sb(trunk, "v_stat", [P, 5, 6])
        v_mv = sb(trunk, "v_mv", [P, 5, 2])
        v_rstd = sb(trunk, "v_rstd", [P, 5])
        vs_t = sb(trunk, "vs_t", [P, BC, NS])
        early = ExitStack()
        v_tok = sb(early, "v_tok", [P, 5, 512])
        cin = sb(early, "cin", [P, BC, WB - 1 + SEQ])
        cin_s = sb(early, "cin_s", [P, BC, NS, WB])
        prod_s = sb(early, "prod_s", [P, BC, NS, WB])
        fac = sb(early, "fac", [P, 2, T])
        early.close()
        late = ExitStack()
        sig = sb(late, "sig", [P, BC, T])
        y_hi = sb(late, "y_hi", [P, BC, T], F32R)
        y_lo = sb(late, "y_lo", [P, BC, T], F32R)
        prod_c = sb(late, "prod_c", [P, NS, WC])
        late.close()
        trunk.close()

        route = ExitStack()
        rt = sb(route, "rt", [P, 3, T])
        hid = sb(route, "hid", [P, 4, T])
        tops = ExitStack()
        top_v = sb(tops, "top_v", [RT_TOK, RT_N, HP, TOPK])
        top_i = sb(tops, "top_i", [RT_TOK, RT_N, HP, TOPK])
        qs = ExitStack()
        keys = sb(qs, "keys", [P, HP, P])
        q_t = sb(qs, "q_t", [P, 2, T])
        score = sb(qs, "score", [RT_TOK, 2, RT_N, P])
        score_r = sb(qs, "score_r", [RT_TOK, RT_N, P])
        pick_v = sb(qs, "pick_v", [RT_TOK, 4, RT_N, TOPK])
        pick_i = sb(qs, "pick_i", [RT_TOK, 4, RT_N, TOPK], U32)
        qs.close()
        cs = ExitStack()
        cand = sb(cs, "cand", [RT_TOK, HEADS, TOPK * TOPK])
        cand_r = sb(cs, "cand_r", [RT_TOK, HEADS, TOPK * TOPK])
        eq = sb(cs, "eq", [RT_TOK, P, TOPK])
        best = sb(cs, "best", [RT_TOK, HEADS, TOPK])
        pos = sb(cs, "pos", [RT_TOK, HEADS * TOPK], U32)
        pos_h = sb(cs, "pos_h", [RT_TOK, 2, HEADS * TOPK], U32)
        pos_f = sb(cs, "pos_f", [RT_TOK, 2, HEADS * TOPK])
        expo = sb(cs, "expo", [RT_TOK, HEADS, TOPK])
        esum = sb(cs, "esum", [RT_TOK, HEADS])
        picked = sb(cs, "picked", [RT_TOK, 3, P])
        cs.close()
        tops.close()
        gs = ExitStack()
        one_i = sb(gs, "one_i", [P, 2, GS, P])
        one_j = sb(gs, "one_j", [P, 2, GS, P])
        gate_buf = sb(gs, "gate_buf", [P, NBLK, GB])
        gs.close()
        route.close()

        down = ExitStack()
        acc = sb(down, "acc", [P, KC, T])
        h_hi = sb(down, "h_hi", [P, 2, 4, T], F32R)
        h_lo = sb(down, "h_lo", [P, 2, 4, T], F32R)
        hid_in = sb(down, "hid_in", [P, 2, 4, T])
        gate_in = sb(down, "gate_in", [P, 2, GBN, 4 * GB])
        down.close()

        pg = ctx.enter_context(nc.psum_tensor("pg", [P, 2, 2, 512], F32))
        pm = ctx.enter_context(nc.psum_tensor("pm", [P, 4, 512], F32))

        raw_in = [sem(f"raw_in{s}") for s in range(4)]
        x_in = sem("x_in")
        par_in = sem("par_in")
        keys_in = sem("keys_in")
        consts = sem("consts")
        passed = sem("passed")
        silu_ready = sem("silu_ready")
        ada_done = sem("ada_done")
        sq_ready, sq_used = sem("sq_ready"), sem("sq_used")
        std_ready, nb_ready, hi_of_nb, a_ready = (sem(n) for n in ("std_ready", "nb_ready", "hi_of_nb", "a_ready"))
        hi_ready, lo_ready = sem("hi_ready"), sem("lo_ready")
        prod = sem("prod")
        pg_free = [sem("pg_free0"), sem("pg_free1")]
        v_prod, v_gelu, v_stats, v_std, v_ready = (sem(n) for n in ("v_prod", "v_gelu", "v_stats", "v_std", "v_ready"))
        trunk_init, mask_done = sem("trunk_init"), sem("mask_done")
        fac_ready, fac_used = sem("fac_ready"), sem("fac_used")
        u_ready = sem("u_ready")
        cin_ready, glu_ready = sem("cin_ready"), sem("glu_ready")
        vt_prod, vt_ready, mix_prod, mix_free = (sem(n) for n in ("vt_prod", "vt_ready", "mix_prod", "mix_free"))
        early_out, late_out = sem("early_out"), sem("late_out")
        conv_pool, conv_ready = sem("conv_pool"), sem("conv_ready")
        src_ready = sem("src_ready")
        yhi_ready, y_ready = sem("yhi_ready"), sem("y_ready")
        sig_ready, sig_used = sem("sig_ready"), sem("sig_used")
        c_sum, c_cent, c_sq, c_sqsum, c_std, c_norm = (sem(n) for n in ("c_sum", "c_cent", "c_sq", "c_sqsum", "c_std", "c_norm"))
        merged_ready, mhi_ready, merged_split = sem("merged_ready"), sem("mhi_ready"), sem("merged_split")
        x_mid, x_done = sem("x_mid"), sem("x_done")
        q_ready, s_prod, s_copied, s_used = (sem(n) for n in ("q_ready", "s_prod", "s_copied", "s_used"))
        e_in, e_out, picks_ready, rt_prod, rt_ready = (sem(n) for n in ("e_in", "e_out", "picks_ready", "rt_prod", "rt_ready"))
        hid_ready = sem("hid_ready")
        hid_out = [sem(f"hid_out{s}") for s in range(4)]
        one_ready, g_prod, g_free, g_full, g_out = (sem(n) for n in ("one_ready", "g_prod", "g_free", "g_full", "g_out"))
        g_stored = sem("g_stored")
        acc_zero = sem("acc_zero")
        down_in = [sem("down_in0"), sem("down_in1")]
        gated, ghi_ready, g_ready = sem("gated"), sem("ghi_ready"), sem("g_ready")
        y_fin, y_done = sem("y_fin"), sem("y_done")
        counts_from_one = [x_done, lo_ready, *pg_free, s_prod, s_copied, *hid_out, g_free, g_stored, rt_ready, rt_prod, g_prod]
        own_act, own_dve, own_pool = sem("own_act"), sem("own_dve"), sem("own_pool")

        def p_(name, rows=slice(0, P)):
            a, b = PAR[name]
            return par[rows, a:b]

        def act_chunk(t, k, h):
            return t[:, k * T + h * HT:k * T + (h + 1) * HT]

        def ring(hi, slot, odd=False):
            if odd:
                return (a_hi if hi else a_lo)[:, slot * D:(slot + 1) * D].rearrange("p (k m) -> p k m", m=P)
            return (w_hi if hi else w_lo)[:, slot]

        PARTS = ((0, 0, HT, 0, HT), (1, 0, H1P, HT, SEQ))

        block = ctx.enter_context(nc.Block())

        @block.sync
        def _(sp):
            for count in counts_from_one:
                sp.sem_inc(count, 1)
            sp.dma_start(x[:, :, :], x_t).then_inc(x_in, 16)
            sp.dma_start(cond[:, :, :], c_t).then_inc(x_in, 16)
            sp.dma_start(fin_g[:, :], final_g).then_inc(x_in, 16)

            def load(l, r, s):
                sp.dma_start(raw[:, s], stream[bass.ds(l * (NMOD + NT) + r, 1)].rearrange("o p k m -> p (o k) m")
                             ).then_inc(raw_in[s], 16)

            with sp.Fori(0, DEPTH) as l:
                for s in range(4):
                    sp.wait_ge(lo_ready, l * NT + 1)
                    load(l, s, s)
                with sp.Fori(1, NMOD // 4) as i:
                    for s in range(4):
                        sp.wait_ge(ada_done, l * NMOD + i * 4 + (s - 3))
                        load(l, i * 4 + s, s)
                for s in range(4):
                    sp.wait_ge(ada_done, l * NMOD + (NMOD - 3 + s))
                    load(l, NMOD + s, s)
                with sp.Fori(1, (T_EU + 8) // 4) as i:
                    for s in range(4):
                        sp.wait_ge(lo_ready, l * NT + i * 4 + (s - 3) + 1)
                        load(l, i * 4 + (NMOD + s), s)
                with sp.Fori(0, NBLK // 4) as i:
                    for s in range(4):
                        sp.wait_ge(lo_ready, l * NT + i * 4 + (T_EU + 8 + s - 3) + 1)
                        load(l, i * 4 + (NMOD + T_EU + 8 + s), s)
                        sp.wait_ge(hid_ready, l * NBLK + i * 4 + (s + 1))
                        sp.dma_start(hidden_dram[:, bass.ds(i * 4 + s, 1), :].rearrange("p o t -> p (o t)"), hid[:, s, :]).then_inc(hid_out[s], 16)
                with sp.Fori((T_ED + 8) // 4, NT // 4) as i:
                    for s in range(4):
                        sp.wait_ge(lo_ready, l * NT + i * 4 + (s - 3) + 1)
                        load(l, i * 4 + (NMOD + s), s)
            sp.wait_ge(y_fin, KC)
            sp.dma_start(y_out, x[:, :, :]).then_inc(y_done, 16)
            sp.wait_ge(y_done, 16)

        @block.gpsimd
        def _(pool):
            own = Steps(pool, own_pool)
            own.do(pool.memset(ident[:, :], 0.0))
            own.do(pool.memset(ones[:, :], 1.0))
            own.do(pool.memset(eps_t[:, :], EPS))
            own.do(pool.iota(iota_u[:, :], pattern=[[1, P]], base=0, channel_multiplier=0))
            own.settle()
            own.do(pool.affine_select(out=ident[:, :], in_=ident[:, :], compare_op=ALU.not_equal, fill=1.0,
                                      base=0, pattern=[[-1, P]], channel_multiplier=1))
            own.do(pool.tensor_copy(iota_f[:, :], iota_u[:, :]))
            own.settle()
            pool.sem_inc(consts, 1)
            own.restart()
            with pool.Fori(0, DEPTH) as l:
                pool.wait_ge(x_done, l + 1)
                pool.sem_inc(passed, 1)
                pool.dma_start(par[:, :], params[bass.ds(l, 1)].rearrange("o p n -> p (o n)")).then_inc(par_in, 16)
                for c in range(BC):
                    pool.dma_start(glu_s[:, c, :, 0:WC - 1], hist_c[bass.ds(l, 1)].rearrange(
                        "o p c s w -> p (o c) s w")[:, c]).then_inc(par_in, 16)
                    pool.dma_start(cin_s[:, c, :, 0:WB - 1], hist_b[bass.ds(l, 1)].rearrange(
                        "o p c s w -> p (o c) s w")[:, c]).then_inc(par_in, 16)
                own.do(pool.memset(cin[:, :, 0:WB - 1], 0.0))
                own.do(pool.memset(glu[:, :, 0:WC - 1], 0.0))
                own.settle()
                pool.sem_inc(trunk_init, 1)
                pool.wait_ge(par_in, (l + 1) * (16 * (1 + 2 * BC)))
                pool.sem_inc(passed, 1)
                w_s = p_("w_s").rearrange("p (g t) -> p g t", g=BC)
                own.do(pool.affine_select(out=w_s, in_=w_s, compare_op=ALU.is_ge, fill=0.0, base=0,
                                          pattern=[[0, BC], [1, P]], channel_multiplier=-1))
                own.settle()
                pool.sem_inc(mask_done, 1)
                pool.wait_ge(v_ready, l + 1)
                pool.sem_inc(passed, 1)
                pool.dma_start(v_out[bass.ds(l, 1)].rearrange("o s d -> (o s) d"), v_tok[P - NS:P, 4, :]).then_inc(early_out, 16)
                pool.wait_ge(cin_ready, l + 1)
                pool.sem_inc(passed, 1)
                pool.dma_start(hb_p[bass.ds(l, 1)].rearrange("o p c w -> p (o c) w"), cin[:, :, SEQ:SEQ + WB - 1]).then_inc(early_out, 16)
                for c in range(BC):
                    pool.dma_start(hb_s[bass.ds(l, 1)].rearrange("o p c s w -> p (o c) s w")[:, c], cin_s[:, c, :, 1:WB]).then_inc(early_out, 16)
                pool.wait_ge(glu_ready, l + 1)
                pool.sem_inc(passed, 1)
                pool.dma_start(hc_p[bass.ds(l, 1)].rearrange("o p c w -> p (o c) w"), glu[:, :, SEQ:SEQ + WC - 1]).then_inc(late_out, 16)
                for c in range(BC):
                    pool.dma_start(hc_s[bass.ds(l, 1)].rearrange("o p c s w -> p (o c) s w")[:, c], glu_s[:, c, :, 1:WC]).then_inc(late_out, 16)
                c = BC - 1
                w_c = p_("conv_c").rearrange("p (c w) -> p c w", c=BC)
                own.link(pool.tensor_scalar(ys[:, 2, c, 0:SEQ], glu[:, c, 0:SEQ], w_c[:, c, 0:1],
                                            p_("conv_c_b")[:, c:c + 1], ALU.mult, ALU.add))
                for k in range(1, WC):
                    own.link(pool.tensor_scalar(pool_tmp[:, :], glu[:, c, k:k + SEQ], w_c[:, c, k:k + 1], None, ALU.mult))
                    own.link(pool.tensor_tensor(ys[:, 2, c, 0:SEQ], ys[:, 2, c, 0:SEQ], pool_tmp[:, :], ALU.add))
                pool.sem_inc(conv_pool, 1)
                own.restart()
                pool.wait_ge(a_ready, l * 2 + 2)
                pool.wait_ge(late_out, (l + 1) * (16 * (1 + BC)))
                pool.sem_inc(passed, 1)
                pool.dma_start(keys[:, :, :], sub_keys[bass.ds(l, 1)].rearrange("o p h n -> p (o h) n")).then_inc(keys_in, 16)
                with pool.Fori(0, GBN) as i:
                    pool.wait_ge(g_full, l * GBN + i + 1)
                    pool.sem_inc(passed, 1)
                    pool.dma_start(gate_dram[bass.ds(i, 1)].rearrange("o p j t -> p (o j t)"),
                                   gate_buf[:, :, :].rearrange("p j t -> p (j t)")).then_inc(g_out, 16)
                    pool.wait_ge(g_out, (l * GBN + i + 1) * 16)
                    pool.sem_inc(g_stored, 1)
                for s in range(4):
                    pool.wait_ge(hid_out[s], (l + 1) * (16 * NBLK // 4) + 1)
                pool.sem_inc(passed, 1)

                def load_group(g, b):
                    pool.dma_start(hid_in[:, b], hidden_dram[:, bass.ds(g * 4, 4), :]).then_inc(down_in[b], 16)
                    pool.dma_start(gate_in[:, b], gate_dram.rearrange("b p j t -> p b (j t)")[:, :, bass.ds(g * (4 * GB), 4 * GB)]
                                   ).then_inc(down_in[b], 16)

                load_group(0, 0)
                load_group(1, 1)
                own.link(pool.memset(acc[:, :, :], 0.0))
                pool.sem_inc(acc_zero, 1)
                own.restart()
                with pool.Fori(1, 16) as i:
                    for b in range(2):
                        pool.wait_ge(g_ready, l * 32 + i * 2 + (b - 1))
                        pool.sem_inc(passed, 1)
                        load_group(i * 2 + b, b)
            pool.wait_ge(early_out, DEPTH * 16 * (2 + BC))
            pool.wait_ge(late_out, DEPTH * 16 * (1 + BC))

        @block.scalar
        def _(act):
            own = Steps(act, own_act)

            def split(l, q, k, slot=None, odd=False):
                s = k % 4
                act.wait_ge(raw_in[s], (l * RAW_PER_SLOT + q + (NMOD // 4 + 1 + k // 4)) * 16)
                act.copy(ring(True, s, odd), raw[:, s]).then_inc(hi_ready, 1)

            def read_product(l, m, g, dst, func, **kw):
                act.wait_ge(prod, l * NM + m)
                for h in range(2):
                    own.do(act.activation(dst(h), pg[:, g % 2, h, 0:HT], func, **kw))
                own.settle()
                act.sem_inc(pg_free[g % 2], 1)

            def squares(l, base, src):
                for k in range(KC):
                    if k >= 2:
                        act.wait_ge(sq_used, l * (2 * KC) + (base * KC + k - 1))
                    own.link(act.activation(sq[:, k % 2, :], src(k), ACT.Square))
                    act.sem_inc(sq_ready, 1)

            def std(l, base, scale):
                act.wait_ge(sq_used, l * (2 * KC) + (base + 1) * KC)
                for h in range(2):
                    own.do(act.activation(rstd[:, h * HT:(h + 1) * HT], pm[:, h, 0:HT], ACT.Sqrt, bias=eps_t[:, 0:1], scale=scale))
                own.settle()
                act.sem_inc(std_ready, 1)

            def modulate(l, w, between):
                shift = 3 * KC * w
                for k in range(KC):
                    act.wait_ge(nb_ready, l * (2 * KC) + (w * KC + k + 1))
                    own.link(act.activation(nb[:, k % 2, 0:SEQ], nb[:, k % 2, 0:SEQ], ACT.Identity,
                                            bias=mod[:, shift + k, 0:1], scale=mod_scale[:, w, k, 0:1]))
                    own.link(act.copy(a_hi[:, k * T:(k + 1) * T], nb[:, k % 2, :]))
                    act.sem_inc(hi_of_nb, 1)
                    between(k)

            act.wait_ge(x_in, 48)
            act.wait_ge(consts, 1)
            own.link(act.activation(cond_silu[:, :, :], cond[:, :, :], ACT.Silu))
            act.sem_inc(silu_ready, 1)
            own.restart()
            with act.Fori(0, DEPTH) as l:
                act.wait_ge(x_done, l + 1)
                squares(l, 0, lambda k: x[:, k, :])
                std(l, 0, 1.0 / D)
                modulate(l, 0, lambda k: split(l, 0, k // 2) if k % 2 else None)
                own.restart()
                act.wait_ge(trunk_init, l + 1)
                for t in range(5):
                    if t < 4:
                        act.wait_ge(v_prod, l * 4 + (t + 1))
                    else:
                        act.wait_ge(prod, l * NM + 4)
                    own.link(act.activation(v_tok[:, t, :], pm[:, t % 4, :], ACT.Gelu_apprx_tanh))
                    act.sem_inc(v_gelu, 1)
                for k in range(4):
                    split(l, 1, k)
                act.wait_ge(v_stats, l + 1)
                own.link(act.activation(v_rstd[:, :], v_mv[:, :, 1], ACT.Sqrt, bias=eps_t[:, 0:1]))
                act.sem_inc(v_std, 1)
                for c in range(BC):
                    read_product(l, T_U + c + 1, c, lambda h, c=c: ys[:, 1, c, h * HT:(h + 1) * HT], ACT.Gelu_apprx_tanh)
                    split(l, 2, c)
                act.sem_inc(u_ready, 1)
                for c in range(BC):
                    n = T_B + 2 * c
                    if c >= 2:
                        act.wait_ge(fac_used, l * 8 + (c - 1))
                    read_product(l, n + 1, 0, lambda h, c=c: fac[:, c % 2, h * HT:(h + 1) * HT], ACT.Copy)
                    act.sem_inc(fac_ready, 1)
                    split(l, 1, 8 + 2 * c)
                    act.wait_ge(prod, l * NM + (n + 2))
                    split(l, 1, 8 + 2 * c + 1)
                for c in range(BC):
                    n = T_C + 2 * c
                    act.wait_ge(fac_used, l * 8 + (c + 3))
                    read_product(l, n + 1, 0, lambda h, c=c: fac[:, c % 2, h * HT:(h + 1) * HT], ACT.Sigmoid)
                    act.sem_inc(fac_ready, 1)
                    split(l, 1, 16 + 2 * c)
                    if c == 0:
                        act.wait_ge(vt_prod, l + 1)
                        for g in range(BC):
                            own.do(act.copy(vs_t[:, g, :], pm[:, 0, g * P + P - NS:g * P + P]))
                        own.settle()
                        act.sem_inc(vt_ready, 1)
                    act.wait_ge(prod, l * NM + (n + 2))
                    split(l, 1, 16 + 2 * c + 1)
                for c in range(BC):
                    act.wait_ge(prod, l * NM + (T_BB + c + 1))
                    split(l, 7, c)
                own.restart()
                act.wait_ge(early_out, (l + 1) * (16 * (2 + BC)))
                act.wait_ge(src_ready, l * 3 + 2)
                for b in range(3):
                    for step in range(12):
                        n = T_BR + 12 * b + step
                        is_gate = step < 4 or 6 <= step < 10
                        if is_gate:
                            d = step if step < 4 else step - 2
                            m = M_BR + 16 * b + (d if d < 4 else d + 4)
                            if b or d >= 4:
                                act.wait_ge(sig_used, l * 24 + (8 * b + d - 3))
                            read_product(l, m + 1, m, lambda h, d=d: sig[:, d % 4, h * HT:(h + 1) * HT], ACT.Sigmoid)
                            act.sem_inc(sig_ready, 1)
                        else:
                            q = (step - 4) if step < 6 else step - 8
                            m = M_BR + 16 * b + (4 + 2 * q if q < 2 else 8 + 2 * q)
                            act.wait_ge(prod, l * NM + (m + 2))
                        split(l, 0, n + 4)
                        if step == 2:
                            act.wait_ge(src_ready, l * 3 + (b + 1))
                            own.link(act.copy(y_hi[:, :, :], ys[:, b, :, :]))
                            act.sem_inc(yhi_ready, 1)
                        if b == 1 and step == 8:
                            act.wait_ge(c_cent, l + 1)
                            for c in range(BC):
                                if c >= 2:
                                    act.wait_ge(c_sqsum, l * BC + (c - 1))
                                own.link(act.activation(sq[:, c % 2, :], ys[:, 2, c, :], ACT.Square))
                                act.sem_inc(c_sq, 1)
                        if b == 1 and step == 10:
                            act.wait_ge(c_sqsum, (l + 1) * BC)
                            for h in range(2):
                                own.do(act.activation(rstd[:, h * HT:(h + 1) * HT], pm[:, 2 + h, 0:HT], ACT.Sqrt,
                                                      bias=eps_t[:, 0:1], scale=1.0 / 512))
                            own.settle()
                            act.sem_inc(c_std, 1)
                        if b == 1 and step == 11:
                            act.wait_ge(c_norm, l + 1)
                            for c in range(BC):
                                own.do(act.activation(ys[:, 2, c, :], ys[:, 2, c, :], ACT.Silu,
                                                      bias=p_("ln_c_b")[:, c:c + 1], scale=p_("ln_c_g")[:, c:c + 1]))
                            own.settle()
                            act.sem_inc(src_ready, 1)
                    own.restart()
                for k in range(KC):
                    act.wait_ge(merged_ready, l * KC + (k + 1))
                    own.link(act.copy(a_hi[:, k * T:(k + 1) * T], merged[:, k, :]))
                    act.sem_inc(mhi_ready, 1)
                with act.Fori(0, 2) as i:
                    for s in range(4):
                        act.wait_ge(prod, l * NM + i * 4 + (M_O + s + 1))
                        split(l, i, T_O + 4 + s)
                act.wait_ge(x_mid, (l + 1) * KC)
                squares(l, 1, lambda k: x[:, k, :])
                std(l, 1, 1.0 / D)
                modulate(l, 1, lambda k: None)
                own.restart()
                act.wait_ge(keys_in, (l + 1) * 16)

                def take_scores(l, i, s):
                    act.wait_ge(s_prod, l * HP + i * 4 + (s + 1) + 1)
                    act.wait_ge(s_used, l * (HP + 2) + i * 4 + (s + 1))
                    b = 2 * (s % 2)
                    own.do(act.copy(score[:, s % 2, 0:4, :], pm[0:RT_TOK, b, :].rearrange("p (t n) -> p t n", t=4)))
                    own.do(act.copy(score[:, s % 2, 4, :], pm[0:RT_TOK, b + 1, 0:P]))
                    own.settle()
                    act.sem_inc(s_copied, 1)

                with act.Fori(0, HP // 4) as i:
                    for s in range(4):
                        act.wait_ge(s_prod, l * HP + i * 4 + (s - 1 if s >= 1 else 0) + 1)
                        read_product(l, i * 4 + (M_Q + s + 1), s, lambda h, s=s: q_t[:, s % 2, h * HT:(h + 1) * HT], ACT.Copy)
                        act.sem_inc(q_ready, 1)
                        split(l, i, T_Q + 4 + s)
                        if s:
                            take_scores(l, i, s - 1)
                    take_scores(l, i, 3)
                    own.restart()

                def up(l, i, k):
                    s = k % 4
                    act.wait_ge(hid_out[s], (l * (NBLK // 4) + i + k // 4) * 16 + 1)
                    read_product(l, i * 4 + (M_EU + k + 1), k, lambda h, s=s: hid[:, s, h * HT:(h + 1) * HT], ACT.Gelu_apprx_tanh)
                    act.sem_inc(hid_ready, 1)
                    split(l, i, T_EU + 4 + k)

                with act.Fori(0, RT_N) as i:
                    for k in range(12):
                        up(l, i * 3, k)
                        if k == 7:
                            act.wait_ge(e_in, l * RT_N + i + 1)
                            own.link(act.activation(expo[:, :, :], expo[:, :, :], ACT.Exp))
                            act.sem_inc(e_out, 1)
                    act.wait_ge(rt_prod, l * RT_N + i + 1 + 1)
                    own.do(act.copy(rt[:, :, bass.ds(i * RT_TOK, RT_TOK)],
                                    pm[:, 0, 0:3 * RT_TOK].rearrange("p (c t) -> p c t", c=3)))
                    own.settle()
                    act.sem_inc(rt_ready, 1)
                    own.restart()
                with act.Fori(0, GBN) as i:
                    for k in range(4):
                        up(l, i + 3 * RT_N, k)
                        act.wait_ge(g_prod, l * (4 * GBN + 1) + i * 4 + (k + 2) + 1)
                        if k == 0:
                            act.wait_ge(g_stored, l * GBN + i + 1)
                        for q, n in ((0, 4), (1, 4), (2, 2)):
                            t0 = k * GS + 4 * q
                            own.do(act.copy(gate_buf[:, :, t0:t0 + n],
                                            pm[:, q, 0:n * P].rearrange("p (t j) -> p j t", t=n)))
                        own.settle()
                        act.sem_inc(g_free, 1)
                    act.sem_inc(g_full, 1)
                    own.restart()
                with act.Fori(3 * RT_N + GBN, NBLK // 4) as i:
                    for k in range(4):
                        up(l, i, k)
                    own.restart()

                def gated_hi(l, g, b):
                    act.wait_ge(gated, l * 32 + g + 1)
                    own.link(act.copy(h_hi[:, b], hid_in[:, b]))
                    act.sem_inc(ghi_ready, 1)

                def group(l, i, b):
                    act.wait_ge(prod, l * NM + i * 16 + (M_ED + 8 * b + 1))
                    for s in range(4):
                        split(l, i * 2, T_ED + 4 * (b + 1) + s, odd=b == 0)
                    gated_hi(l, i * 2 + (b + 1), 1 - b)

                gated_hi(l, 0, 0)
                own.restart()
                with act.Fori(0, 15) as i:
                    group(l, i, 0)
                    group(l, i, 1)
                    own.restart()
                group(l, 15, 0)
                own.restart()
            act.wait_ge(x_done, DEPTH + 1)
            squares(DEPTH, 0, lambda k: x[:, k, :])
            std(DEPTH, 0, 1.0 / D)

        @block.vector
        def _(dve):
            own = Steps(dve, own_dve)
            tt = dve.tensor_tensor

            def split(l, m, s, odd=False):
                dve.wait_ge(hi_ready, l * NT + m + 1)
                tt(ring(False, s, odd), raw[:, s], ring(True, s, odd).bitcast(F32), ALU.subtract).then_inc(lo_ready, 1)

            def take(l, m):
                dve.wait_ge(prod, l * NM + m)

            def release(g):
                own.settle()
                dve.sem_inc(pg_free[g % 2], 1)

            def spread(t, n, size):
                return t.unsqueeze(2).to_broadcast([t.shape[0], t.shape[1], n])

            def norm(l, w, between):
                dve.wait_ge(std_ready, l * 2 + (w + 1))
                own.link(dve.reciprocal(rstd[:, :], rstd[:, :]))
                shift = 3 * KC * w

                def low(k):
                    dve.wait_ge(hi_of_nb, l * (2 * KC) + (w * KC + k + 1))
                    own.link(tt(a_lo[:, k * T:(k + 1) * T], nb[:, k % 2, :], a_hi[:, k * T:(k + 1) * T].bitcast(F32), ALU.subtract))

                for k in range(KC):
                    own.link(tt(nb[:, k % 2, :], x[:, k, :], rstd[:, :], ALU.mult))
                    own.link(tt(nb[:, k % 2, SEQ:T], nb[:, k % 2, SEQ:T], mod_scale[:, w, k, 1:NC], ALU.mult))
                    own.link(tt(nb[:, k % 2, SEQ:T], nb[:, k % 2, SEQ:T], mod[:, shift + k, 1:NC], ALU.add))
                    dve.sem_inc(nb_ready, 1)
                    if k:
                        low(k - 1)
                    between(k)
                low(KC - 1)
                dve.sem_inc(a_ready, 1)

            dve.wait_ge(consts, 1)
            dve.wait_ge(x_in, 48)
            with dve.Fori(0, DEPTH) as l:
                dve.wait_ge(x_done, l + 1)
                dve.wait_ge(ada_done, (l + 1) * NMOD)
                dve.wait_ge(par_in, (l + 1) * (16 * (1 + 2 * BC)))
                own.link(tt(mod[:, :, :], pm[:, 2, 0:NMOD * NC].rearrange("p (m c) -> p m c", c=NC),
                            spread(p_("ada_b"), NC, NMOD), ALU.add))
                for w in range(2):
                    at = KC + 3 * KC * w
                    own.link(dve.tensor_scalar(mod_scale[:, w], mod[:, at:at + KC, :], 1.0, None, ALU.add))
                    own.link(tt(mod_scale[:, w], mod_scale[:, w], spread(p_("norm_g")[:, w * KC:(w + 1) * KC], NC, KC), ALU.mult))
                norm(l, 0, lambda k: split(l, k // 2, k // 2) if k % 2 and k < KC - 1 else None)
                split(l, 3, 3)
                own.restart()
                for t in range(5):
                    dve.wait_ge(v_gelu, l * 5 + (t + 1))
                    own.link(dve.bn_stats(v_stat[:, t, :], v_tok[:, t, :]))
                    own.link(dve.bn_aggr(v_mv[:, t, :], v_stat[:, t, :]))
                dve.sem_inc(v_stats, 1)
                for s in range(4):
                    split(l, 4 + s, s)
                dve.wait_ge(v_std, l + 1)
                own.link(dve.reciprocal(v_rstd[:, :], v_rstd[:, :]))
                for c in range(BC):
                    for t in ((0, 1), (2, 3), (4,), ())[c]:
                        own.do(dve.tensor_scalar(v_tok[:, t, :], v_tok[:, t, :], v_mv[:, t, 0:1], v_rstd[:, t:t + 1],
                                                 ALU.subtract, ALU.mult))
                    own.settle()
                    if c >= 2:
                        wide = p_(("ln_a_g", "ln_a_b")[c - 2]).unsqueeze(1).to_broadcast([P, 5, 512])
                        own.link(tt(v_tok[:, :, :], v_tok[:, :, :], wide, (ALU.mult, ALU.add)[c - 2]))
                    split(l, T_B + c, c)
                dve.sem_inc(v_ready, 1)

                def times_factor(l, n, c, wide, narrow, w, count):
                    dve.wait_ge(fac_ready, l * 8 + (count + 1))
                    take(l, n + 1)
                    g = n % 2
                    own.do(tt(wide[:, c, w - 1:w - 1 + HT], pg[:, g, 0, 0:HT], fac[:, c % 2, 0:HT], ALU.mult))
                    own.do(tt(wide[:, c, w - 1 + HT:w - 1 + SEQ], pg[:, g, 1, 0:H1P], fac[:, c % 2, HT:SEQ], ALU.mult))
                    own.do(tt(narrow[:, c, :, w - 1], pg[:, g, 1, H1P:HT], fac[:, c % 2, SEQ:T], ALU.mult))
                    release(g)
                    dve.sem_inc(fac_used, 1)

                dve.wait_ge(trunk_init, l + 1)
                for c in range(BC):
                    n = T_B + 2 * c
                    split(l, n + 4, 0 if c % 2 == 0 else 2)
                    times_factor(l, n + 1, c, cin, cin_s, WB, c)
                    split(l, n + 5, 1 if c % 2 == 0 else 3)
                dve.sem_inc(cin_ready, 1)

                w_b = p_("conv_b").rearrange("p (c w) -> p c w", c=BC)

                def conv_b(c):
                    own.link(dve.tensor_scalar(ys[:, 0, c, 0:SEQ], cin[:, c, 0:SEQ], w_b[:, c, 0:1], None, ALU.mult))
                    for k in range(1, WB):
                        own.link(dve.scalar_tensor_tensor(out=ys[:, 0, c, 0:SEQ], in0=cin[:, c, k:k + SEQ], scalar=w_b[:, c, k:k + 1],
                                                          in1=ys[:, 0, c, 0:SEQ], op0=ALU.mult, op1=ALU.add))

                def conv_b_samples():
                    for c in range(BC):
                        own.do(tt(prod_s[:, c], cin_s[:, c], w_b[:, c, :].unsqueeze(1).to_broadcast([P, NS, WB]), ALU.mult))
                    own.settle()
                    for c in range(BC):
                        own.do(dve.tensor_reduce(ys[:, 0, c, SEQ:T], prod_s[:, c], AX_X, ALU.add))
                    own.settle()

                def mix(l, g, first):
                    dve.wait_ge(mix_prod, l * BC + (first + 1))
                    own.link(tt(mix_t[:, :].rearrange("p (c t) -> p c t", c=4), pm[:, g, :].rearrange("p (c t) -> p c t", c=4),
                                p_("b_s")[:, g * P:(g + 1) * P].unsqueeze(1).to_broadcast([P, 4, P]), ALU.add))
                    own.do(tt(ys[:, 1, g, 0:SEQ], mix_t[:, :], ys[:, 1, g, 0:SEQ], ALU.mult))
                    own.do(dve.tensor_scalar(tmp8[:, :], vs_t[:, g, :], p_("w_s00")[:, g:g + 1], p_("b_s")[:, g * P:g * P + 1],
                                             ALU.mult, ALU.add))
                    own.settle()
                    own.link(tt(ys[:, 1, g, SEQ:T], ys[:, 1, g, SEQ:T], tmp8[:, :], ALU.mult))

                dve.wait_ge(u_ready, l + 1)
                for c in range(BC):
                    n = T_C + 2 * c
                    split(l, n + 4, 0 if c % 2 == 0 else 2)
                    conv_b(c)
                    times_factor(l, n + 1, c, glu, glu_s, WC, 4 + c)
                    split(l, n + 5, 1 if c % 2 == 0 else 3)
                    if c == 1:
                        dve.wait_ge(vt_ready, l + 1)
                    if c >= 1:
                        mix(l, c, c - 1)
                    else:
                        conv_b_samples()
                dve.sem_inc(glu_ready, 1)
                mix(l, 0, 3)

                w_c = p_("conv_c").rearrange("p (c w) -> p c w", c=BC)
                taps = [(c, k) for c in range(BC - 1) for k in range(WC)]

                def conv_c(n):
                    for c, k in [taps.pop(0) for _ in range(min(n, len(taps)))]:
                        if k == 0:
                            own.link(dve.tensor_scalar(ys[:, 2, c, 0:SEQ], glu[:, c, 0:SEQ], w_c[:, c, 0:1],
                                                       p_("conv_c_b")[:, c:c + 1], ALU.mult, ALU.add))
                        else:
                            own.link(dve.scalar_tensor_tensor(out=ys[:, 2, c, 0:SEQ], in0=glu[:, c, k:k + SEQ], scalar=w_c[:, c, k:k + 1],
                                                              in1=ys[:, 2, c, 0:SEQ], op0=ALU.mult, op1=ALU.add))

                def conv_c_samples(c):
                    own.link(tt(prod_c[:, :, :], glu_s[:, c], w_c[:, c, :].unsqueeze(1).to_broadcast([P, NS, WC]), ALU.mult))
                    own.link(dve.tensor_reduce(tmp8[:, :], prod_c[:, :, :], AX_X, ALU.add))
                    own.link(dve.tensor_scalar(ys[:, 2, c, SEQ:T], tmp8[:, :], p_("conv_c_b")[:, c:c + 1], None, ALU.add))

                for c in range(BC):
                    take(l, T_BB + c + 1)
                    for h in range(2):
                        s_ = slice(h * HT, (h + 1) * HT)
                        own.do(tt(ys[:, 0, c, s_], pg[:, c % 2, h, 0:HT], ys[:, 0, c, s_], ALU.mult))
                    release(c)
                    split(l, T_BB + 4 + c, c)
                    conv_c(3)
                dve.sem_inc(src_ready, 2)
                own.restart()

                def centre_c():
                    dve.wait_ge(c_sum, l + 1)
                    for h in range(2):
                        own.do(dve.tensor_scalar(nb[:, 0, h * HT:(h + 1) * HT], pm[:, h, 0:HT], 1.0 / 512, None, ALU.mult))
                    own.settle()
                    for c in range(BC):
                        own.do(tt(ys[:, 2, c, :], ys[:, 2, c, :], nb[:, 0, :], ALU.subtract))
                    own.settle()
                    dve.sem_inc(c_cent, 1)

                def normalise_c():
                    dve.wait_ge(c_std, l + 1)
                    own.link(dve.reciprocal(rstd[:, :], rstd[:, :]))
                    for c in range(BC):
                        own.do(tt(ys[:, 2, c, :], ys[:, 2, c, :], rstd[:, :], ALU.mult))
                    own.settle()
                    dve.sem_inc(c_norm, 1)

                dve.wait_ge(early_out, (l + 1) * (16 * (2 + BC)))
                for b in range(3):
                    for step in range(12):
                        n = T_BR + 12 * b + step
                        if not (step < 4 or 6 <= step < 10):
                            q = (step - 4) if step < 6 else step - 8
                            for d in (2 * q, 2 * q + 1):
                                m = M_BR + 16 * b + (4 + d if d < 4 else 8 + d)
                                dve.wait_ge(sig_ready, l * 24 + (8 * b + d + 1))
                                take(l, m + 1)
                                for h in range(2):
                                    s_ = slice(h * HT, (h + 1) * HT)
                                    own.do(tt(merged[:, d, s_] if b == 0 else sig[:, d % 4, s_], pg[:, m % 2, h, 0:HT],
                                              sig[:, d % 4, s_], ALU.mult))
                                release(m)
                                if b:
                                    own.link(tt(merged[:, d, :], merged[:, d, :], sig[:, d % 4, :], ALU.add))
                                dve.sem_inc(sig_used, 1)
                                if b == 2:
                                    dve.sem_inc(merged_ready, 1)
                        split(l, n + 4, step % 4)
                        if step == 2:
                            dve.wait_ge(yhi_ready, l * 3 + (b + 1))
                            own.link(tt(y_lo[:, :, :], ys[:, b, :, :], y_hi[:, :, :].bitcast(F32), ALU.subtract))
                            dve.sem_inc(y_ready, 1)
                        if b == 0 or b == 1 and step < 4:
                            conv_c(5 + (step % 2))
                        if b == 1 and step == 4:
                            conv_c(99)
                            for c in range(BC):
                                conv_c_samples(c)
                            dve.wait_ge(conv_pool, l + 1)
                            dve.sem_inc(conv_ready, 1)
                        if b == 1 and step == 7:
                            centre_c()
                        if b == 1 and step == 11:
                            normalise_c()
                    own.restart()
                for k in range(KC):
                    dve.wait_ge(mhi_ready, l * KC + (k + 1))
                    own.link(tt(a_lo[:, k * T:(k + 1) * T], merged[:, k, :], a_hi[:, k * T:(k + 1) * T].bitcast(F32), ALU.subtract))
                dve.sem_inc(merged_split, 1)
                own.restart()

                for k in range(KC):
                    gate = mod[:, 2 * KC + k, :]
                    take(l, M_O + k + 1)
                    own.do(tt(tmp8[:, :], pg[:, k % 2, 1, H1P:HT], gate[:, 1:NC], ALU.mult))
                    for h, a, b_, ta, tb in PARTS:
                        own.do(dve.scalar_tensor_tensor(out=x[:, k, ta:tb], in0=pg[:, k % 2, h, a:b_], scalar=gate[:, 0:1],
                                                        in1=x[:, k, ta:tb], op0=ALU.mult, op1=ALU.add))
                    own.settle()
                    own.link(tt(x[:, k, SEQ:T], x[:, k, SEQ:T], tmp8[:, :], ALU.add))
                    release(k)
                    dve.sem_inc(x_mid, 1)
                    split(l, T_O + 4 + k, k % 4)
                own.restart()
                norm(l, 1, lambda k: None)
                own.restart()

                def tops_of(l, i, s):
                    dve.wait_ge(s_copied, l * HP + i * 4 + (s + 1) + 1)
                    dve.sem_inc(passed, 1)
                    sc = score[:, s % 2]
                    for t in range(RT_N):
                        own.do(dve.max(pick_v[:, s, t, 0:8], sc[:, t, :]))
                    own.settle()
                    for t in range(RT_N):
                        own.do(dve.max_index(pick_i[:, s, t, 0:8], pick_v[:, s, t, 0:8], sc[:, t, :]))
                        own.do(dve.match_replace(score_r[:, t, :], pick_v[:, s, t, 0:8], sc[:, t, :], NEG))
                    own.settle()
                    dve.sem_inc(s_used, 1)
                    for t in range(RT_N):
                        own.do(dve.max(pick_v[:, s, t, 8:16], score_r[:, t, :]))
                    own.settle()
                    for t in range(RT_N):
                        own.do(dve.max_index(pick_i[:, s, t, 8:16], pick_v[:, s, t, 8:16], score_r[:, t, :]))
                    own.settle()

                dve.sem_inc(s_used, 2)
                with dve.Fori(0, HP // 4) as i:
                    for s in range(4):
                        split(l, i * 4 + (T_Q + 4 + s), s)
                        if s:
                            tops_of(l, i, s - 1)
                    tops_of(l, i, 3)
                    for s in range(4):
                        own.do(dve.tensor_copy(top_v[:, :, bass.ds(i * 4 + s, 1), :].rearrange("p t o k -> p t (o k)"), pick_v[:, s]))
                        own.do(dve.tensor_copy(top_i[:, :, bass.ds(i * 4 + s, 1), :].rearrange("p t o k -> p t (o k)"), pick_i[:, s]))
                    own.settle()
                    own.restart()

                dve.wait_ge(rt_ready, l * RT_N + 1)
                dve.sem_inc(passed, 1)
                iota16 = iota_f[0:RT_TOK, 0:TOPK].unsqueeze(1).to_broadcast([RT_TOK, P, TOPK])

                def of_tile(t, i):
                    return t[:, bass.ds(i, 1)].rearrange("p o (h z) k -> p (o h) z k", z=2)

                def each_head(f):
                    for h in range(HEADS):
                        own.do(f(h))
                    own.settle()

                def route_piece(l, i, k):
                    shape = [RT_TOK, HEADS, TOPK, TOPK]
                    if k == 0:
                        v = of_tile(top_v, i)
                        own.link(tt(cand[:, :, :].rearrange("p h (a b) -> p h a b", a=TOPK),
                                    v[:, :, 0, :].unsqueeze(3).to_broadcast(shape), v[:, :, 1, :].unsqueeze(2).to_broadcast(shape), ALU.add))
                    if k == 1:
                        each_head(lambda h: dve.max(best[:, h, 0:8], cand[:, h, :]))
                    if k == 2:
                        each_head(lambda h: dve.max_index(pos[:, h * TOPK:h * TOPK + 8], best[:, h, 0:8], cand[:, h, :]))
                    if k == 3:
                        each_head(lambda h: dve.match_replace(cand_r[:, h, :], best[:, h, 0:8], cand[:, h, :], NEG))
                    if k == 4:
                        each_head(lambda h: dve.max(best[:, h, 8:16], cand_r[:, h, :]))
                    if k == 5:
                        own.link(tt(expo[:, :, :], best[:, :, :], best[:, :, 0:1].to_broadcast([RT_TOK, HEADS, TOPK]), ALU.subtract))
                        dve.sem_inc(e_in, 1)
                        each_head(lambda h: dve.max_index(pos[:, h * TOPK + 8:h * TOPK + 16], best[:, h, 8:16], cand_r[:, h, :]))
                    if k == 6:
                        own.do(dve.tensor_scalar(pos_h[:, 0], pos[:, :], 4, None, ALU.logical_shift_right))
                        own.do(dve.tensor_scalar(pos_h[:, 1], pos[:, :], 15, None, ALU.bitwise_and))
                        own.settle()
                        own.link(dve.tensor_copy(pos_f[:, :, :], pos_h[:, :, :]))
                    if k in (7, 9):
                        z = (k - 7) // 2
                        own.link(tt(eq[:, :, :], iota16, pos_f[:, z, :].unsqueeze(2).to_broadcast([RT_TOK, P, TOPK]), ALU.is_equal))
                    if k in (8, 10):
                        z = (k - 8) // 2
                        dve.wait_ge(rt_prod, l * RT_N + i + 1)
                        e4 = eq[:, :, :].rearrange("p (h k) a -> p h k a", h=HEADS)
                        own.link(tt(e4, e4, of_tile(top_i, i)[:, :, z, :].unsqueeze(2).to_broadcast(shape), ALU.mult))
                        own.link(dve.tensor_reduce(picked[:, z, :], eq[:, :, :], AX_X, ALU.add))
                    if k == 11:
                        dve.wait_ge(e_out, l * RT_N + i + 1)
                        own.link(dve.tensor_reduce(esum[:, :], expo[:, :, :], AX_X, ALU.add))
                        own.link(dve.reciprocal(esum[:, :], esum[:, :]))
                        own.link(tt(picked[:, 2, :].rearrange("p (h k) -> p h k", h=HEADS), expo[:, :, :],
                                    esum[:, :].unsqueeze(2).to_broadcast([RT_TOK, HEADS, TOPK]), ALU.mult))
                        dve.sem_inc(picks_ready, 1)

                with dve.Fori(0, RT_N) as i:
                    for k in range(12):
                        route_piece(l, i, k)
                        split(l, i * 12 + (T_EU + 4 + k), k % 4)
                    own.restart()

                iota_b = iota_f[:, :].unsqueeze(1).to_broadcast([P, GS, P])
                dve.wait_ge(rt_ready, (l + 1) * RT_N + 1)
                dve.sem_inc(passed, 1)
                dve.sem_inc(g_prod, 1)
                with dve.Fori(0, GBN) as i:
                    for k in range(4):
                        def picks(c):
                            return rt[:, c, bass.ds(i * GB + k * GS, GS)].unsqueeze(2).to_broadcast([P, GS, P])
                        dve.wait_ge(g_prod, l * (4 * GBN + 1) + i * 4 + k + 1)
                        own.do(tt(one_i[:, k % 2], iota_b, picks(0), ALU.is_equal))
                        own.do(tt(one_j[:, k % 2], iota_b, picks(1), ALU.is_equal))
                        own.settle()
                        own.link(tt(one_j[:, k % 2], one_j[:, k % 2], picks(2), ALU.mult))
                        dve.sem_inc(one_ready, 1)
                        split(l, i * 4 + (T_EU + 12 * RT_N + 4 + k), k)
                    own.restart()
                with dve.Fori(T_EU // 4 + 3 * RT_N + GBN, T_ED // 4) as i:
                    for k in range(4):
                        split(l, i * 4 + (4 + k), k)

                def gate_times_hidden(l, i, b):
                    dve.wait_ge(down_in[b], (l * 16 + i + 1) * 32)
                    own.link(tt(hid_in[:, b].rearrange("p j (b t) -> p j b t", t=GB), hid_in[:, b].rearrange("p j (b t) -> p j b t", t=GB),
                                gate_in[:, b].rearrange("p b (j t) -> p j b t", t=GB), ALU.mult))
                    dve.sem_inc(gated, 1)

                def gated_lo(l, g, b):
                    dve.wait_ge(ghi_ready, l * 32 + g + 1)
                    own.link(tt(h_lo[:, b], hid_in[:, b], h_hi[:, b].bitcast(F32), ALU.subtract))
                    dve.sem_inc(g_ready, 1)

                def group(l, i, b, last=False):
                    for d in range(KC):
                        take(l, i * 16 + (M_ED + 8 * b + d + 1))
                        for h in range(2):
                            s_ = slice(h * HT, (h + 1) * HT)
                            own.do(tt(acc[:, d, s_], acc[:, d, s_], pg[:, d % 2, h, 0:HT], ALU.add))
                        release(d)
                        if last:
                            continue
                        if d == 0:
                            gate_times_hidden(l, i + b, 1 - b)
                        if 1 <= d <= 4:
                            split(l, i * 8 + (T_ED + 4 * (b + 1) + d - 1), d - 1, odd=b == 0)
                        if d == 5:
                            gated_lo(l, i * 2 + (b + 1), 1 - b)

                dve.wait_ge(acc_zero, l + 1)
                gate_times_hidden(l, 0, 0)
                gated_lo(l, 0, 0)
                own.restart()
                with dve.Fori(0, 15) as i:
                    group(l, i, 0)
                    group(l, i, 1)
                    own.restart()
                group(l, 15, 0)
                group(l, 15, 1, last=True)
                for k in range(KC):
                    gate = mod[:, 5 * KC + k, :]
                    own.do(dve.scalar_tensor_tensor(out=x[:, k, 0:SEQ], in0=acc[:, k, 0:SEQ], scalar=gate[:, 0:1],
                                                    in1=x[:, k, 0:SEQ], op0=ALU.mult, op1=ALU.add))
                    own.link(tt(acc[:, k, SEQ:T], acc[:, k, SEQ:T], gate[:, 1:NC], ALU.mult))
                    own.link(tt(x[:, k, SEQ:T], x[:, k, SEQ:T], acc[:, k, SEQ:T], ALU.add))
                dve.sem_inc(x_done, 1)
                own.restart()
            dve.wait_ge(std_ready, 2 * DEPTH + 1)
            own.link(dve.reciprocal(rstd[:, :], rstd[:, :]))
            for k in range(KC):
                own.link(dve.scalar_tensor_tensor(out=x[:, k, :], in0=x[:, k, :], scalar=fin_g[:, k:k + 1], in1=rstd[:, :],
                                                  op0=ALU.mult, op1=ALU.mult))
                dve.sem_inc(y_fin, 1)

        @block.tensor
        def _(pe):
            def three(out, w, a, k, first, last):
                pe.matmul(out, w[0], a[0], start=first, stop=False)
                pe.matmul(out, w[0], a[1], start=False, stop=False)
                return pe.matmul(out, w[1], a[0], start=False, stop=last)

            def weights(l, m):
                pe.wait_ge(lo_ready, l * NT + m + 1 + 1)

            def buffer(l, g, parity):
                pe.wait_ge(pg_free[parity], l * NG + g + 1)

            def chunk(k, h):
                return act_chunk(a_hi, k, h), act_chunk(a_lo, k, h)

            def product(parity, s, rhs, ks=range(KC)):
                for h in range(2):
                    for n, k in enumerate(ks):
                        mm = three(pg[:, parity, h, 0:HT], (w_hi[:, s, k, :], w_lo[:, s, k, :]), rhs(n, h), k, n == 0, n == len(ks) - 1)
                mm.then_inc(prod, 1)

            def squares_sum(l, base):
                for k in range(KC):
                    pe.wait_ge(sq_ready, l * (2 * KC) + (base * KC + k + 1))
                    for h in range(2):
                        mm = pe.matmul(pm[:, h, 0:HT], ones[:, :], sq[:, k % 2, h * HT:(h + 1) * HT], start=k == 0, stop=k == KC - 1)
                    mm.then_inc(sq_used, 1)

            pe.wait_ge(consts, 1)
            pe.wait_ge(silu_ready, 1)
            with pe.Fori(0, DEPTH) as l:
                pe.wait_ge(x_done, l + 1)
                squares_sum(l, 0)
                with pe.Fori(0, NMOD // 4) as i:
                    for s in range(4):
                        pe.wait_ge(raw_in[s], (l * RAW_PER_SLOT + i + 1) * 16)
                        for k in range(KC):
                            mm = pe.matmul(pm[:, 2, bass.ds((i * 4 + s) * NC, NC)], raw[:, s, k, :], cond_silu[:, k, :],
                                           start=k == 0, stop=k == KC - 1)
                        mm.then_inc(ada_done, 1)
                pe.wait_ge(a_ready, l * 2 + 1)
                weights(l, 3)
                for t in range(5):
                    t0 = t * P if t < 4 else T - P
                    if t == 4:
                        pe.wait_ge(v_gelu, l * 5 + 1)
                    for k in range(KC):
                        tok = slice(k * T + t0, k * T + t0 + P)
                        hi, lo = w_hi[:, :, k, :], w_lo[:, :, k, :]
                        out = pm[:, t % 4, :]
                        pe.matmul(out, a_hi[:, tok], hi, start=k == 0, stop=False)
                        pe.matmul(out, a_hi[:, tok], lo, start=False, stop=False)
                        mm = pe.matmul(out, a_lo[:, tok], hi, start=False, stop=k == KC - 1)
                    if t < 4:
                        mm.then_inc(v_prod, 1)
                    else:
                        mm.then_inc(prod, 4)
                with pe.Fori(1, 4) as i:
                    for s in range(4):
                        weights(l, i * 4 + s)
                        buffer(l, i * 2 + (s // 2 - 2), s % 2)
                        product(s % 2, s, chunk)
                pe.wait_ge(v_ready, l + 1)
                pe.wait_ge(mask_done, l + 1)
                for g in range(BC):
                    mm = pe.transpose(pm[:, 0, g * P:(g + 1) * P], v_tok[:, 4, g * P:(g + 1) * P], ident[:, :])
                mm.then_inc(vt_prod, 1)
                for g in (1, 2, 3):
                    for c in range(4):
                        mm = pe.matmul(pm[:, g, c * P:(c + 1) * P], v_tok[:, c, g * P:(g + 1) * P],
                                       p_("w_s")[:, g * P:(g + 1) * P], start=True, stop=True)
                    mm.then_inc(mix_prod, 1)
                with pe.Fori(4, 6) as i:
                    for s in range(4):
                        weights(l, i * 4 + s)
                        buffer(l, i * 2 + (s // 2 - 2), s % 2)
                        product(s % 2, s, chunk)
                pe.wait_ge(vt_ready, l + 1)
                for c in range(4):
                    mm = pe.matmul(pm[:, 0, c * P:(c + 1) * P], v_tok[:, c, 0:P], p_("w_s")[:, 0:P], start=True, stop=True)
                mm.then_inc(mix_prod, 1)
                for s in range(4):
                    weights(l, T_BB + s)
                    buffer(l, (T_BB - 4 + s) // 2, s % 2)
                    product(s % 2, s, chunk)
                for b in range(3):
                    for step in range(12):
                        s = step % 4
                        weights(l, T_BR + 12 * b + step)
                        if step < 4 or 6 <= step < 10:
                            d = step if step < 4 else step - 2
                            g = G_BR + 16 * b + (d if d < 4 else d + 4)
                            buffer(l, g // 2, g % 2)
                            product(g % 2, s, chunk)
                        else:
                            q = (step - 4) if step < 6 else step - 8
                            if q == 0:
                                pe.wait_ge(y_ready, l * 3 + (b + 1))
                            for e in range(2):
                                d = 2 * q + e
                                g = G_BR + 16 * b + (4 + d if d < 4 else 8 + d)
                                buffer(l, g // 2, g % 2)
                                product(g % 2, s, lambda n, h: (y_hi[:, n, h * HT:(h + 1) * HT], y_lo[:, n, h * HT:(h + 1) * HT]),
                                        range(4 * e, 4 * e + 4))
                        if b == 1 and step == 6:
                            pe.wait_ge(conv_ready, l + 1)
                            for c in range(BC):
                                for h in range(2):
                                    mm = pe.matmul(pm[:, h, 0:HT], ones[:, :], ys[:, 2, c, h * HT:(h + 1) * HT], start=c == 0, stop=c == BC - 1)
                            mm.then_inc(c_sum, 1)
                        if b == 1 and step == 9:
                            for c in range(BC):
                                pe.wait_ge(c_sq, l * BC + (c + 1))
                                for h in range(2):
                                    mm = pe.matmul(pm[:, 2 + h, 0:HT], ones[:, :], sq[:, c % 2, h * HT:(h + 1) * HT], start=c == 0, stop=c == BC - 1)
                                mm.then_inc(c_sqsum, 1)
                pe.wait_ge(merged_split, l + 1)
                pe.sem_inc(passed, 1)
                with pe.Fori(0, 2) as i:
                    for s in range(4):
                        weights(l, i * 4 + (T_O + s))
                        buffer(l, i * 2 + (G_O // 2 + s // 2), s % 2)
                        product(s % 2, s, chunk)
                squares_sum(l, 1)
                pe.wait_ge(a_ready, l * 2 + 2)
                pe.wait_ge(keys_in, (l + 1) * 16)
                pe.sem_inc(passed, 1)

                def scores(l, i, s):
                    pe.wait_ge(q_ready, l * HP + i * 4 + (s + 1))
                    pe.wait_ge(s_copied, l * HP + i * 4 + (s - 1 if s >= 1 else 0) + 1)
                    for t in range(RT_N):
                        b, c = 2 * (s % 2) + t // 4, (t % 4) * P
                        mm = pe.matmul(pm[0:RT_TOK, b, c:c + P], q_t[:, s % 2, t * RT_TOK:(t + 1) * RT_TOK],
                                       keys[:, bass.ds(i * 4 + s, 1), :].rearrange("p o n -> p (o n)"), start=True, stop=True)
                    mm.then_inc(s_prod, 1)

                with pe.Fori(0, HP // 4) as i:
                    for s in range(4):
                        weights(l, i * 4 + (T_Q + s))
                        buffer(l, i * 2 + (G_Q // 2 + s // 2), s % 2)
                        product(s % 2, s, chunk)
                        if s:
                            scores(l, i, s - 1)
                    scores(l, i, 3)

                def up(l, i, k):
                    weights(l, i * 4 + (T_EU + k))
                    buffer(l, i * 2 + (G_EU // 2 + k // 2), k % 2)
                    product(k % 2, k % 4, chunk)

                with pe.Fori(0, RT_N) as i:
                    for k in range(12):
                        up(l, i * 3, k)
                    pe.wait_ge(picks_ready, l * RT_N + i + 1)
                    pe.wait_ge(rt_ready, l * RT_N + i + 1)
                    for c in range(3):
                        mm = pe.transpose(pm[:, 0, c * RT_TOK:(c + 1) * RT_TOK], picked[:, c, :], ident[0:RT_TOK, 0:RT_TOK])
                    mm.then_inc(rt_prod, 1)
                pe.wait_ge(rt_ready, (l + 1) * RT_N + 1)
                pe.sem_inc(passed, 1)
                with pe.Fori(0, GBN) as i:
                    for k in range(4):
                        up(l, i + 3 * RT_N, k)
                        pe.wait_ge(one_ready, l * (4 * GBN) + i * 4 + (k + 1))
                        pe.wait_ge(g_free, l * (4 * GBN) + i * 4 + k + 1)
                        for t in range(GS):
                            mm = pe.matmul(pm[:, t // 4, (t % 4) * P:(t % 4 + 1) * P], one_i[:, k % 2, t, :], one_j[:, k % 2, t, :],
                                           start=True, stop=True)
                        mm.then_inc(g_prod, 1)
                with pe.Fori(3 * RT_N + GBN, NBLK // 4) as i:
                    for k in range(4):
                        up(l, i, k)

                def group(l, i, b):
                    weights(l, i * 8 + (T_ED + 4 * b + 3))
                    pe.wait_ge(g_ready, l * 32 + i * 2 + (b + 1))
                    for d in range(KC):
                        buffer(l, i * 8 + (G_ED // 2 + 4 * b + d // 2), d % 2)
                        for h in range(2):
                            for j in range(4):
                                w = ring(True, j, b == 1)[:, d, :], ring(False, j, b == 1)[:, d, :]
                                a = h_hi[:, b, j, h * HT:(h + 1) * HT], h_lo[:, b, j, h * HT:(h + 1) * HT]
                                mm = three(pg[:, d % 2, h, 0:HT], w, a, j, j == 0, j == 3)
                        mm.then_inc(prod, 1)

                with pe.Fori(0, 16) as i:
                    group(l, i, 0)
                    group(l, i, 1)
            pe.wait_ge(x_done, DEPTH + 1)
            squares_sum(DEPTH, 0)


def _lay_out(i, np):
    L = DEPTH

    def tiles(w):
        k, m = w.shape
        return w.reshape(k // P, P, m // P, P).transpose(2, 1, 0, 3)

    def channels(a):
        return np.moveaxis(a.reshape(*a.shape[:-1], -1, P), (-1, -2), (0, 1))

    def wide(a):
        return np.broadcast_to(a.reshape(1, -1), (P, a.size))

    stream = np.empty((L, NMOD + NT, P, KC, P), np.float32)
    params = np.empty((L, P, NPAR), np.float32)
    for l in range(L):
        s = stream[l]
        s[0:NMOD] = tiles(i["ada_w"][l])
        t = s[NMOD:]
        w_in = tiles(i["w_in"][l])
        u, v, hb, bb, cb, ac, gc = (w_in[4 * n:4 * n + 4] for n in range(7))
        t[T_V:T_V + 4], t[T_U:T_U + 4] = v, u
        t[T_B:T_C:2], t[T_B + 1:T_C:2] = hb, cb
        t[T_C:T_BB:2], t[T_C + 1:T_BB:2] = gc, ac
        t[T_BB:T_BR] = bb
        for b, r in enumerate((1, 0, 2)):
            n = T_BR + 12 * b
            gates = w_in[28 + 8 * r:36 + 8 * r]
            br = tiles(i["w_branch"][l, r]).reshape(4, 2, P, BC, P).transpose(0, 2, 1, 3, 4).reshape(4, P, KC, P)
            t[n:n + 4], t[n + 4:n + 6], t[n + 6:n + 10], t[n + 10:n + 12] = gates[0:4], br[0:2], gates[4:8], br[2:4]
        t[T_O:T_Q] = tiles(i["w_out"][l])
        t[T_Q:T_EU] = tiles(i["peer_w_query"][l])
        t[T_EU:T_ED] = i["peer_u"][l].reshape(P, NBLK, KC, P).transpose(1, 3, 2, 0)
        t[T_ED:NT] = i["peer_v"][l].reshape(P, NBLK, KC, P).transpose(1, 0, 2, 3)

        def put(name, a):
            params[l][:, PAR[name][0]:PAR[name][1]] = a.reshape(P, -1)

        put("ada_b", channels(i["ada_b"][l]))
        put("norm_g", channels(i["norm_g"][l]).transpose(0, 2, 1))
        put("ln_a_g", wide(i["ln_a_g"][l]))
        put("ln_a_b", wide(i["ln_a_b"][l]))
        put("w_s", i["w_spatial"][l].transpose(2, 0, 1))
        put("b_s", wide(i["b_spatial"][l]))
        put("w_s00", wide(i["w_spatial"][l, :, 0, 0]))
        put("conv_b", channels(i["conv_b_w"][l]))
        put("conv_c", channels(i["conv_c_w"][l]))
        for name, key in (("conv_c_b", "conv_c_b"), ("ln_c_g", "ln_c_g"), ("ln_c_b", "ln_c_b")):
            put(name, channels(i[key][l]))
    tokens = np.concatenate([i["x_prompt"].reshape(SEQ, D), i["x_sample"].reshape(NS, D)])
    cond = np.concatenate([i["c_prompt"], i["c_sample"]])

    def history(a):
        l, s, w, c = a.shape
        return a.reshape(l, s, w, c // P, P).transpose(0, 4, 3, 1, 2)

    return {
        "stream": stream, "x_t": channels(tokens), "c_t": channels(cond), "final_g": channels(i["final_g"]),
        "params": params, "hist_b": history(i["state_conv_b"]), "hist_c": history(i["state_conv_c"]),
        "sub_keys": i["peer_sub_keys"].transpose(0, 4, 1, 2, 3).reshape(L, P, HP, P),
    }


_OUTS = {
    "y_out": (P, KC, T), "v_out": (DEPTH, NS, 512), "hb_p": (DEPTH, P, BC, WB - 1), "hb_s": (DEPTH, P, BC, NS, WB - 1),
    "hc_p": (DEPTH, P, BC, WC - 1), "hc_s": (DEPTH, P, BC, NS, WC - 1),
}


def kernel(**inputs):
    import numpy as np
    import concourse.bacc as bacc
    from concourse.bass_utils import run_bass_kernel_spmd

    arrays = {k: np.ascontiguousarray(v) for k, v in _lay_out({k: np.asarray(v) for k, v in inputs.items()}, np).items()}
    nc = bacc.Bacc("TRN2", target_bir_lowering=False, num_devices=1)
    args = {k: nc.dram_tensor(k, a.shape, mybir.dt.from_np(a.dtype), kind="ExternalInput").ap() for k, a in arrays.items()}
    args |= {k: nc.dram_tensor(k, s, F32, kind="ExternalOutput").ap() for k, s in _OUTS.items()}
    build(nc, **args)
    r = run_bass_kernel_spmd(nc, [arrays], core_ids=[0]).results[0]
    y = np.asarray(r["y_out"]).transpose(2, 1, 0).reshape(T, D)

    def rows(a):
        a = np.moveaxis(np.asarray(a), (2, 1), (-2, -1))
        return np.ascontiguousarray(a.reshape(*a.shape[:-2], -1))

    return (np.ascontiguousarray(y[:SEQ]).reshape(1, SEQ, D), np.ascontiguousarray(y[SEQ:]).reshape(NS, 1, D),
            np.asarray(r["v_out"]).reshape(DEPTH, NS, 1, 512), rows(r["hb_p"])[:, None], rows(r["hb_s"]),
            rows(r["hc_p"])[:, None], rows(r["hc_s"]))
```

```python
from contextlib import ExitStack

import concourse.bass as bass
from concourse import mybir

F32 = mybir.dt.float32
F32R = mybir.dt.float32r
U32 = mybir.dt.uint32
ALU = mybir.AluOpType
ACT = mybir.ActivationFunctionType
AX_X = mybir.AxisListType.X

P = 128
D = 1024
KC = D // P
SEQ = 512
NS = 8
T = SEQ + NS
HT = T // 2
H1P = SEQ - HT
NC = 1 + NS
DEPTH = 2
BC = 4
WB, WC = 3, 31
EPS = 1e-6
NMOD = 6 * KC
HEADS, TOPK = 8, 16
HP = 2 * HEADS
NBLK = 128
RT_TOK, RT_N = 104, 5
GB = 40
GBN = T // GB
GS = 10
NEG = -3.0e38

T_V, T_U, T_B, T_C, T_BB, T_BR, T_O, T_Q, T_EU, T_ED = 0, 4, 8, 16, 24, 28, 64, 72, 88, 216
NT = T_ED + NBLK
RAW_PER_SLOT = (NMOD + NT) // 4
ADA_1 = 2 * KC
ADA_AT = (1, 2, 3, 6, 7, 8, 9, 10)
assert ADA_1 + 4 * len(ADA_AT) == NMOD
M_BR, M_O, M_Q, M_EU, M_ED = 28, 76, 84, 100, 228
NM = M_ED + 8 * 32
G_BR, G_O, G_Q, G_EU, G_ED = 24, 72, 80, 96, 224
NG = (G_ED + 8 * 32) // 2
PAR = {}
_at = 0
for _n, _w in (("ln_a_g", 512), ("ln_a_b", 512), ("w_s", 512),
               ("b_s", 512), ("w_s00", BC), ("conv_b", BC * WB), ("conv_c", BC * WC),
               ("conv_c_b", BC), ("ln_c_g", BC), ("ln_c_b", BC)):
    PAR[_n] = (_at, _at + _w)
    _at += _w
NPAR = _at


class Steps:

    def __init__(self, eng, sem):
        self.eng, self.sem, self.n = eng, sem, 0

    def do(self, ins):
        ins.then_inc(self.sem, 1)
        self.n += 1

    def settle(self):
        self.eng.wait_ge(self.sem, self.n)

    def link(self, ins):
        self.do(ins)
        self.settle()

    def restart(self):
        if self.n:
            self.settle()
            self.eng.sem_clear(self.sem)
            self.n = 0


def ring_turn(q):
    return ADA_1 // 4 + q + 1 + sum(i + 1 <= q for i in ADA_AT)


def build(nc, stream, x_t, c_t, final_g, ada_params, params, hist_b, hist_c, sub_keys,
          y_out, v_out, hb_p, hb_s, hc_p, hc_s):
    hidden_dram = nc.dram_tensor("hidden_dram", (P, NBLK, T), F32).ap()
    gate_dram = nc.dram_tensor("gate_dram", (GBN, P, NBLK, GB), F32).ap()
    stream = stream.rearrange("l n p k m -> (l n) p k m")
    with ExitStack() as ctx:

        def sb(stack, name, shape, dt=F32):
            return stack.enter_context(nc.sbuf_tensor(name, shape, dt))

        def sem(name):
            return ctx.enter_context(nc.semaphore(name))

        raw = sb(ctx, "raw", [P, 4, KC, P])
        w_hi = sb(ctx, "w_hi", [P, 4, KC, P], F32R)
        w_lo = sb(ctx, "w_lo", [P, 4, KC, P], F32R)
        a_hi = sb(ctx, "a_hi", [P, KC * T], F32R)
        a_lo = sb(ctx, "a_lo", [P, KC * T], F32R)
        x = sb(ctx, "x", [P, KC, T])
        par = sb(ctx, "par", [P, NPAR])
        cond = sb(ctx, "cond", [P, KC, NC])
        ada_par = sb(ctx, "ada_par", [P, DEPTH, NMOD + 2 * KC])
        ada_row = sb(ctx, "ada_row", [NC, 512])
        cond_silu = sb(ctx, "cond_silu", [P, KC, NC])
        mod = sb(ctx, "mod", [P, NMOD, NC])
        mod_scale = sb(ctx, "mod_scale", [P, 2, KC, NC])
        fin_g = sb(ctx, "fin_g", [P, KC])
        ident = sb(ctx, "ident", [P, P])
        ones = sb(ctx, "ones", [P, P])
        iota_u = sb(ctx, "iota_u", [P, P], U32)
        iota_f = sb(ctx, "iota_f", [P, P])
        eps_t = sb(ctx, "eps_t", [P, 1])
        tmp8 = sb(ctx, "tmp8", [P, NS])

        trunk = ExitStack()
        sq = sb(trunk, "sq", [P, 2, T])
        rstd = sb(trunk, "rstd", [P, T])
        mean = sb(trunk, "mean", [P, T])
        merged = sb(trunk, "merged", [P, KC, T])
        glu = sb(trunk, "glu", [P, BC, WC - 1 + SEQ])
        glu_s = sb(trunk, "glu_s", [P, BC, NS, WC])
        ys = sb(trunk, "ys", [P, 3, BC, T])
        pool_tmp = sb(trunk, "pool_tmp", [P, SEQ])
        mix_t = sb(trunk, "mix_t", [P, SEQ])
        v_stat = sb(trunk, "v_stat", [P, 5, 6])
        v_mv = sb(trunk, "v_mv", [P, 5, 2])
        v_rstd = sb(trunk, "v_rstd", [P, 5])
        vs_t = sb(trunk, "vs_t", [P, BC, NS])
        early = ExitStack()
        v_tok = sb(early, "v_tok", [P, 5, 512])
        cin = sb(early, "cin", [P, BC, WB - 1 + SEQ])
        cin_s = sb(early, "cin_s", [P, BC, NS, WB])
        prod_s = sb(early, "prod_s", [P, BC, NS, WB])
        fac = sb(early, "fac", [P, 2, T])
        early.close()
        late = ExitStack()
        sig = sb(late, "sig", [P, BC, T])
        y_hi = sb(late, "y_hi", [P, BC, T], F32R)
        y_lo = sb(late, "y_lo", [P, BC, T], F32R)
        prod_c = sb(late, "prod_c", [P, NS, WC])
        late.close()
        trunk.close()

        route = ExitStack()
        rt = sb(route, "rt", [P, 3, T])
        hid = sb(route, "hid", [P, 4, T])
        tops = ExitStack()
        top_v = sb(tops, "top_v", [RT_TOK, RT_N, HP, TOPK])
        top_i = sb(tops, "top_i", [RT_TOK, RT_N, HP, TOPK])
        qs = ExitStack()
        keys = sb(qs, "keys", [P, HP, P])
        q_t = sb(qs, "q_t", [P, 2, T])
        score = sb(qs, "score", [RT_TOK, 2, RT_N, P])
        score_r = sb(qs, "score_r", [RT_TOK, RT_N, P])
        pick_v = sb(qs, "pick_v", [RT_TOK, 4, RT_N, TOPK])
        pick_i = sb(qs, "pick_i", [RT_TOK, 4, RT_N, TOPK], U32)
        qs.close()
        cs = ExitStack()
        cand = sb(cs, "cand", [RT_TOK, HEADS, TOPK * TOPK])
        cand_r = sb(cs, "cand_r", [RT_TOK, HEADS, TOPK * TOPK])
        eq = sb(cs, "eq", [RT_TOK, P, TOPK])
        best = sb(cs, "best", [RT_TOK, HEADS, TOPK])
        pos = sb(cs, "pos", [RT_TOK, HEADS * TOPK], U32)
        pos_h = sb(cs, "pos_h", [RT_TOK, 2, HEADS * TOPK], U32)
        pos_f = sb(cs, "pos_f", [RT_TOK, 2, HEADS * TOPK])
        expo = sb(cs, "expo", [RT_TOK, HEADS, TOPK])
        esum = sb(cs, "esum", [RT_TOK, HEADS])
        picked = sb(cs, "picked", [RT_TOK, 3, P])
        cs.close()
        tops.close()
        gs = ExitStack()
        one_i = sb(gs, "one_i", [P, 2, GS, P], F32R)
        one_j = sb(gs, "one_j", [P, 2, 2, GS, P], F32R)
        eq_j = sb(gs, "eq_j", [P, 2, GS, P])
        g_hi = sb(gs, "g_hi", [P, T], F32R)
        g_lo = sb(gs, "g_lo", [P, T])
        gate_buf = sb(gs, "gate_buf", [P, NBLK, GB])
        gs.close()
        route.close()

        down = ExitStack()
        acc = sb(down, "acc", [P, KC, T])
        h_hi = sb(down, "h_hi", [P, 2, 4, T], F32R)
        h_lo = sb(down, "h_lo", [P, 2, 4, T], F32R)
        hid_in = sb(down, "hid_in", [P, 2, 4, T])
        gate_in = sb(down, "gate_in", [P, 2, GBN, 4 * GB])
        down.close()

        pg = ctx.enter_context(nc.psum_tensor("pg", [P, 2, 2, 512], F32))
        pm = ctx.enter_context(nc.psum_tensor("pm", [P, 4, 512], F32))

        raw_in = [sem(f"raw_in{s}") for s in range(4)]
        x_in = sem("x_in")
        par_in = sem("par_in")
        keys_in = sem("keys_in")
        consts = sem("consts")
        passed = sem("passed")
        silu_ready = sem("silu_ready")
        ada_done, ada_row_ready, ada_prod, mod_taken = (sem(n) for n in ("ada_done", "ada_row_ready", "ada_prod", "mod_taken"))
        sq_ready, sq_used = sem("sq_ready"), sem("sq_used")
        std_ready, nb_ready, hi_of_nb, a_ready = (sem(n) for n in ("std_ready", "nb_ready", "hi_of_nb", "a_ready"))
        hi_ready, lo_ready = sem("hi_ready"), sem("lo_ready")
        prod = sem("prod")
        pg_free = [sem("pg_free0"), sem("pg_free1")]
        v_prod, v_gelu, v_stats, v_std, v_ready = (sem(n) for n in ("v_prod", "v_gelu", "v_stats", "v_std", "v_ready"))
        trunk_init, mask_done = sem("trunk_init"), sem("mask_done")
        fac_ready, fac_used = sem("fac_ready"), sem("fac_used")
        u_ready = sem("u_ready")
        cin_ready, glu_ready = sem("cin_ready"), sem("glu_ready")
        vt_prod, vt_ready, mix_prod, mix_free = (sem(n) for n in ("vt_prod", "vt_ready", "mix_prod", "mix_free"))
        early_out, late_out = sem("early_out"), sem("late_out")
        conv_pool, conv_ready = sem("conv_pool"), sem("conv_ready")
        src_ready = sem("src_ready")
        yhi_ready, y_ready = sem("yhi_ready"), sem("y_ready")
        sig_ready, sig_used = sem("sig_ready"), sem("sig_used")
        c_sum, c_cent, c_sq, c_sqsum, c_std, c_norm = (sem(n) for n in ("c_sum", "c_cent", "c_sq", "c_sqsum", "c_std", "c_norm"))
        merged_ready, mhi_ready, merged_split = sem("merged_ready"), sem("mhi_ready"), sem("merged_split")
        x_mid, x_done = sem("x_mid"), sem("x_done")
        q_ready, s_prod, s_copied, s_used = (sem(n) for n in ("q_ready", "s_prod", "s_copied", "s_used"))
        e_in, e_out, picks_ready, rt_prod, rt_ready = (sem(n) for n in ("e_in", "e_out", "picks_ready", "rt_prod", "rt_ready"))
        hid_ready = sem("hid_ready")
        hid_out = [sem(f"hid_out{s}") for s in range(4)]
        one_ready, g_prod, g_free, g_out = (sem(n) for n in ("one_ready", "g_prod", "g_free", "g_out"))
        ghi_of_picks, eq_ready, one_lo_ready = sem("ghi_of_picks"), sem("eq_ready"), sem("one_lo_ready")
        acc_zero = sem("acc_zero")
        down_in = [sem("down_in0"), sem("down_in1")]
        gated, ghi_ready, g_ready = sem("gated"), sem("ghi_ready"), sem("g_ready")
        y_fin, y_done = sem("y_fin"), sem("y_done")
        counts_from_one = [mod_taken, x_done, lo_ready, *pg_free, s_prod, s_copied, *hid_out, g_free, g_out, rt_ready, rt_prod, g_prod]
        own_act, own_dve, own_pool = sem("own_act"), sem("own_dve"), sem("own_pool")

        def p_(name, rows=slice(0, P)):
            a, b = PAR[name]
            return par[rows, a:b]

        def act_chunk(t, k, h):
            return t[:, k * T + h * HT:k * T + (h + 1) * HT]

        def ring(hi, slot, odd=False):
            if odd:
                return (a_hi if hi else a_lo)[:, slot * D:(slot + 1) * D].rearrange("p (k m) -> p k m", m=P)
            return (w_hi if hi else w_lo)[:, slot]

        def samples(t):
            return t[:, :].rearrange("p (k t) -> p k t", k=KC)[:, :, SEQ:T]

        PARTS = ((0, 0, HT, 0, HT), (1, 0, H1P, HT, SEQ))

        block = ctx.enter_context(nc.Block())

        @block.sync
        def _(sp):
            for count in counts_from_one:
                sp.sem_inc(count, 1)
            sp.dma_start(x[:, :, :], x_t).then_inc(x_in, 16)
            sp.dma_start(cond[:, :, :], c_t).then_inc(x_in, 16)
            sp.dma_start(fin_g[:, :], final_g).then_inc(x_in, 16)
            sp.dma_start(ada_par[:, :, :], ada_params).then_inc(x_in, 16)

            def load(l, r, s):
                sp.dma_start(raw[:, s], stream[bass.ds(l * (NMOD + NT) + r, 1)].rearrange("o p k m -> p (o k) m")
                             ).then_inc(raw_in[s], 16)

            with sp.Fori(0, DEPTH) as l:
                for s in range(4):
                    sp.wait_ge(lo_ready, l * NT + 1)
                    load(l, s, s)
                with sp.Fori(1, ADA_1 // 4) as i:
                    sp.wait_ge(ada_done, l * (NMOD // 4) + i)
                    for s in range(4):
                        load(l, i * 4 + s, s)
                sp.wait_ge(ada_done, l * (NMOD // 4) + ADA_1 // 4)
                for s in range(4):
                    load(l, NMOD + s, s)
                for s in range(4):
                    sp.wait_ge(lo_ready, l * NT + (s + 1) + 1)
                    load(l, NMOD + 4 + s, s)
                def batches(first, q0, n):
                    with sp.Fori(0, n) as q:
                        for s in range(4):
                            sp.wait_ge(lo_ready, l * NT + q * 4 + (4 * first - 4 + s + 1) + 1)
                            load(l, q * 4 + (ADA_1 + 4 * q0 + s), s)
                        sp.wait_ge(ada_done, l * (NMOD // 4) + q + (ADA_1 // 4 + q0 + 1))
                        for s in range(4):
                            load(l, q * 4 + (NMOD + 4 * first + s), s)

                batches(2, 0, 3)
                for k in range(8):
                    sp.wait_ge(lo_ready, l * NT + (20 + k - 3) + 1)
                    load(l, NMOD + 20 + k, k % 4)
                batches(7, 3, 5)
                with sp.Fori(12, (T_EU + 8) // 4) as i:
                    for s in range(4):
                        sp.wait_ge(lo_ready, l * NT + i * 4 + (s - 3) + 1)
                        load(l, i * 4 + (NMOD + s), s)
                with sp.Fori(0, NBLK // 4) as i:
                    for s in range(4):
                        sp.wait_ge(lo_ready, l * NT + i * 4 + (T_EU + 8 + s - 3) + 1)
                        load(l, i * 4 + (NMOD + T_EU + 8 + s), s)
                        sp.wait_ge(hid_ready, l * NBLK + i * 4 + (s + 1))
                        sp.dma_start(hidden_dram[:, bass.ds(i * 4 + s, 1), :].rearrange("p o t -> p (o t)"), hid[:, s, :]).then_inc(hid_out[s], 16)
                with sp.Fori((T_ED + 8) // 4, NT // 4) as i:
                    for s in range(4):
                        sp.wait_ge(lo_ready, l * NT + i * 4 + (s - 3) + 1)
                        load(l, i * 4 + (NMOD + s), s)
            sp.wait_ge(y_fin, KC)
            sp.dma_start(y_out, x[:, :, :]).then_inc(y_done, 16)
            sp.wait_ge(y_done, 16)

        @block.gpsimd
        def _(pool):
            own = Steps(pool, own_pool)
            own.do(pool.memset(ident[:, :], 0.0))
            own.do(pool.memset(ones[:, :], 1.0))
            own.do(pool.memset(eps_t[:, :], EPS))
            own.do(pool.iota(iota_u[:, :], pattern=[[1, P]], base=0, channel_multiplier=0))
            own.settle()
            own.do(pool.affine_select(out=ident[:, :], in_=ident[:, :], compare_op=ALU.not_equal, fill=1.0,
                                      base=0, pattern=[[-1, P]], channel_multiplier=1))
            own.do(pool.tensor_copy(iota_f[:, :], iota_u[:, :]))
            own.settle()
            pool.sem_inc(consts, 1)
            own.restart()
            with pool.Fori(0, DEPTH) as l:
                pool.wait_ge(x_done, l + 1)
                pool.sem_inc(passed, 1)
                pool.dma_start(par[:, :], params[bass.ds(l, 1)].rearrange("o p n -> p (o n)")).then_inc(par_in, 16)
                for c in range(BC):
                    pool.dma_start(glu_s[:, c, :, 0:WC - 1], hist_c[bass.ds(l, 1)].rearrange(
                        "o p c s w -> p (o c) s w")[:, c]).then_inc(par_in, 16)
                    pool.dma_start(cin_s[:, c, :, 0:WB - 1], hist_b[bass.ds(l, 1)].rearrange(
                        "o p c s w -> p (o c) s w")[:, c]).then_inc(par_in, 16)
                own.do(pool.memset(cin[:, :, 0:WB - 1], 0.0))
                own.do(pool.memset(glu[:, :, 0:WC - 1], 0.0))
                own.settle()
                pool.sem_inc(trunk_init, 1)
                pool.wait_ge(par_in, (l + 1) * (16 * (1 + 2 * BC)))
                pool.sem_inc(passed, 1)
                w_s = p_("w_s").rearrange("p (g t) -> p g t", g=BC)
                own.do(pool.affine_select(out=w_s, in_=w_s, compare_op=ALU.is_ge, fill=0.0, base=0,
                                          pattern=[[0, BC], [1, P]], channel_multiplier=-1))
                own.settle()
                pool.sem_inc(mask_done, 1)
                pool.wait_ge(v_ready, l + 1)
                pool.sem_inc(passed, 1)
                pool.dma_start(v_out[bass.ds(l, 1)].rearrange("o s d -> (o s) d"), v_tok[P - NS:P, 4, :]).then_inc(early_out, 16)
                pool.wait_ge(cin_ready, l + 1)
                pool.sem_inc(passed, 1)
                pool.dma_start(hb_p[bass.ds(l, 1)].rearrange("o p c w -> p (o c) w"), cin[:, :, SEQ:SEQ + WB - 1]).then_inc(early_out, 16)
                for c in range(BC):
                    pool.dma_start(hb_s[bass.ds(l, 1)].rearrange("o p c s w -> p (o c) s w")[:, c], cin_s[:, c, :, 1:WB]).then_inc(early_out, 16)
                pool.wait_ge(glu_ready, l + 1)
                pool.sem_inc(passed, 1)
                pool.dma_start(hc_p[bass.ds(l, 1)].rearrange("o p c w -> p (o c) w"), glu[:, :, SEQ:SEQ + WC - 1]).then_inc(late_out, 16)
                for c in range(BC):
                    pool.dma_start(hc_s[bass.ds(l, 1)].rearrange("o p c s w -> p (o c) s w")[:, c], glu_s[:, c, :, 1:WC]).then_inc(late_out, 16)
                c = BC - 1
                w_c = p_("conv_c").rearrange("p (c w) -> p c w", c=BC)
                own.link(pool.tensor_scalar(ys[:, 2, c, 0:SEQ], glu[:, c, 0:SEQ], w_c[:, c, 0:1],
                                            p_("conv_c_b")[:, c:c + 1], ALU.mult, ALU.add))
                for k in range(1, WC):
                    own.link(pool.tensor_scalar(pool_tmp[:, :], glu[:, c, k:k + SEQ], w_c[:, c, k:k + 1], None, ALU.mult))
                    own.link(pool.tensor_tensor(ys[:, 2, c, 0:SEQ], ys[:, 2, c, 0:SEQ], pool_tmp[:, :], ALU.add))
                pool.sem_inc(conv_pool, 1)
                own.restart()
                pool.wait_ge(a_ready, l * 2 + 2)
                pool.wait_ge(late_out, (l + 1) * (16 * (1 + BC)))
                pool.sem_inc(passed, 1)
                pool.dma_start(keys[:, :, :], sub_keys[bass.ds(l, 1)].rearrange("o p h n -> p (o h) n")).then_inc(keys_in, 16)
                pool.wait_ge(eq_ready, l * (4 * GBN + 1) + 1)
                pool.sem_inc(passed, 1)
                with pool.Fori(0, GBN) as i:
                    for k in range(4):
                        pool.wait_ge(eq_ready, l * (4 * GBN + 1) + i * 4 + (k + 2))
                        g = g_lo[:, bass.ds(i * GB + k * GS, GS)].unsqueeze(2).to_broadcast([P, GS, P])
                        own.link(pool.tensor_tensor(one_j[:, k % 2, 1], eq_j[:, k % 2], g, ALU.mult))
                        pool.sem_inc(one_lo_ready, 1)
                    own.restart()
                pool.wait_ge(g_out, (l + 1) * (16 * GBN) + 1)
                for s in range(4):
                    pool.wait_ge(hid_out[s], (l * (NBLK // 4) + 2) * 16 + 1)
                pool.sem_inc(passed, 1)

                def load_group(g, b):
                    pool.dma_start(hid_in[:, b], hidden_dram[:, bass.ds(g * 4, 4), :]).then_inc(down_in[b], 16)
                    pool.dma_start(gate_in[:, b], gate_dram.rearrange("b p j t -> p b (j t)")[:, :, bass.ds(g * (4 * GB), 4 * GB)]
                                   ).then_inc(down_in[b], 16)

                load_group(0, 0)
                load_group(1, 1)
                for s in range(4):
                    pool.wait_ge(hid_out[s], (l + 1) * (16 * NBLK // 4) + 1)
                pool.sem_inc(passed, 1)
                own.link(pool.memset(acc[:, :, :], 0.0))
                pool.sem_inc(acc_zero, 1)
                own.restart()
                with pool.Fori(1, 16) as i:
                    for b in range(2):
                        pool.wait_ge(g_ready, l * 32 + i * 2 + (b - 1))
                        pool.sem_inc(passed, 1)
                        load_group(i * 2 + b, b)
            pool.wait_ge(early_out, DEPTH * 16 * (2 + BC))
            pool.wait_ge(late_out, DEPTH * 16 * (1 + BC))

        @block.scalar
        def _(act):
            own = Steps(act, own_act)

            def split(l, q, k, slot=None, odd=False):
                s = k % 4
                turn = ring_turn(q + k // 4) if isinstance(q, int) else q + (NMOD // 4 + 1 + k // 4)
                act.wait_ge(raw_in[s], (l * RAW_PER_SLOT + turn) * 16)
                act.copy(ring(True, s, odd), raw[:, s]).then_inc(hi_ready, 1)

            def read_product(l, m, g, dst, func, **kw):
                act.wait_ge(prod, l * NM + m)
                for h in range(2):
                    own.do(act.activation(dst(h), pg[:, g % 2, h, 0:HT], func, **kw))
                own.settle()
                act.sem_inc(pg_free[g % 2], 1)

            def square(l, base, k):
                if k >= 2:
                    act.wait_ge(sq_used, l * (2 * KC) + (base * KC + k - 1))
                own.link(act.activation(sq[:, k % 2, :], x[:, k, :], ACT.Square))
                act.sem_inc(sq_ready, 1)

            def std(l, base, scale):
                act.wait_ge(sq_used, l * (2 * KC) + (base + 1) * KC)
                for h in range(2):
                    own.do(act.activation(rstd[:, h * HT:(h + 1) * HT], pm[:, h, 0:HT], ACT.Sqrt, bias=eps_t[:, 0:1], scale=scale))
                own.settle()
                act.sem_inc(std_ready, 1)

            def ada_rows(l, n):
                act.wait_ge(ada_done, l * (NMOD // 4) + (n + 1))
                own.link(act.copy(ada_row[:, :], pm[0:NC, 3, :]))
                act.sem_inc(ada_row_ready, 1)

            def modulate(l, w, between):
                shift = 3 * KC * w
                for k in range(KC):
                    act.wait_ge(nb_ready, l * (2 * KC + 2) + (w * (KC + 1) + k + 1))
                    own.link(act.activation(merged[:, k, 0:SEQ], merged[:, k, 0:SEQ], ACT.Identity,
                                            bias=mod[:, shift + k, 0:1], scale=mod_scale[:, w, k, 0:1]))
                    own.link(act.copy(a_hi[:, k * T:k * T + SEQ], merged[:, k, 0:SEQ]))
                    act.sem_inc(hi_of_nb, 1)
                    between(k)
                act.wait_ge(nb_ready, l * (2 * KC + 2) + (w + 1) * (KC + 1))
                own.link(act.copy(samples(a_hi), merged[:, :, SEQ:T]))
                act.sem_inc(hi_of_nb, 1)

            act.wait_ge(x_in, 64)
            act.wait_ge(consts, 1)
            own.link(act.activation(cond_silu[:, :, :], cond[:, :, :], ACT.Silu))
            act.sem_inc(silu_ready, 1)
            own.restart()
            with act.Fori(0, DEPTH) as l:
                act.wait_ge(x_done, l + 1)
                for k in range(KC):
                    square(l, 0, k)
                    if k % 2:
                        ada_rows(l, k // 2)
                std(l, 0, 1.0 / D)
                modulate(l, 0, lambda k: split(l, 0, k // 2) if k % 2 else None)
                own.restart()
                act.wait_ge(trunk_init, l + 1)
                for t in range(5):
                    if t < 4:
                        act.wait_ge(v_prod, l * 4 + (t + 1))
                    else:
                        act.wait_ge(prod, l * NM + 4)
                    own.link(act.activation(v_tok[:, t, :], pm[:, t % 4, :], ACT.Gelu_apprx_tanh))
                    act.sem_inc(v_gelu, 1)
                for k in range(4):
                    split(l, 1, k)
                act.wait_ge(v_stats, l + 1)
                own.link(act.activation(v_rstd[:, :], v_mv[:, :, 1], ACT.Sqrt, bias=eps_t[:, 0:1]))
                act.sem_inc(v_std, 1)
                for c in range(BC):
                    read_product(l, T_U + c + 1, c, lambda h, c=c: ys[:, 1, c, h * HT:(h + 1) * HT], ACT.Gelu_apprx_tanh)
                    if c == 0:
                        ada_rows(l, 4)
                    split(l, 2, c)
                act.sem_inc(u_ready, 1)
                for c in range(BC):
                    n = T_B + 2 * c
                    if c >= 2:
                        act.wait_ge(fac_used, l * 8 + (c - 1))
                    read_product(l, n + 1, 0, lambda h, c=c: fac[:, c % 2, h * HT:(h + 1) * HT], ACT.Copy)
                    act.sem_inc(fac_ready, 1)
                    if c % 2 == 0:
                        ada_rows(l, 5 + c // 2)
                    split(l, 1, 8 + 2 * c)
                    act.wait_ge(prod, l * NM + (n + 2))
                    split(l, 1, 8 + 2 * c + 1)
                for c in range(BC):
                    n = T_C + 2 * c
                    act.wait_ge(fac_used, l * 8 + (c + 3))
                    read_product(l, n + 1, 0, lambda h, c=c: fac[:, c % 2, h * HT:(h + 1) * HT], ACT.Sigmoid)
                    act.sem_inc(fac_ready, 1)
                    split(l, 1, 16 + 2 * c)
                    if c == 0:
                        act.wait_ge(vt_prod, l + 1)
                        for g in range(BC):
                            own.do(act.copy(vs_t[:, g, :], pm[:, 0, g * P + P - NS:g * P + P]))
                        own.settle()
                        act.sem_inc(vt_ready, 1)
                    act.wait_ge(prod, l * NM + (n + 2))
                    split(l, 1, 16 + 2 * c + 1)
                for c in range(BC):
                    act.wait_ge(prod, l * NM + (T_BB + c + 1))
                    if c == 0:
                        ada_rows(l, 7)
                    split(l, 7, c)
                own.restart()
                act.wait_ge(early_out, (l + 1) * (16 * (2 + BC)))
                act.wait_ge(src_ready, l * 3 + 2)
                for b in range(3):
                    for step in range(12):
                        n = T_BR + 12 * b + step
                        is_gate = step < 4 or 6 <= step < 10
                        if is_gate:
                            d = step if step < 4 else step - 2
                            m = M_BR + 16 * b + (d if d < 4 else d + 4)
                            if b or d >= 4:
                                act.wait_ge(sig_used, l * 24 + (8 * b + d - 3))
                            read_product(l, m + 1, m, lambda h, d=d: sig[:, d % 4, h * HT:(h + 1) * HT], ACT.Sigmoid)
                            act.sem_inc(sig_ready, 1)
                        else:
                            q = (step - 4) if step < 6 else step - 8
                            m = M_BR + 16 * b + (4 + 2 * q if q < 2 else 8 + 2 * q)
                            act.wait_ge(prod, l * NM + (m + 2))
                        if step % 4 == 0 and (b == 0 or b == 1 and step == 0):
                            ada_rows(l, 8 + 3 * b + step // 4)
                        split(l, 0, n + 4)
                        if step == 2:
                            act.wait_ge(src_ready, l * 3 + (b + 1))
                            own.link(act.copy(y_hi[:, :, :], ys[:, b, :, :]))
                            act.sem_inc(yhi_ready, 1)
                        if b == 1 and step == 8:
                            act.wait_ge(c_cent, l + 1)
                            for c in range(BC):
                                if c >= 2:
                                    act.wait_ge(c_sqsum, l * BC + (c - 1))
                                own.link(act.activation(sq[:, c % 2, :], ys[:, 2, c, :], ACT.Square))
                                act.sem_inc(c_sq, 1)
                        if b == 1 and step == 10:
                            act.wait_ge(c_sqsum, (l + 1) * BC)
                            for h in range(2):
                                own.do(act.activation(rstd[:, h * HT:(h + 1) * HT], pm[:, 2 + h, 0:HT], ACT.Sqrt,
                                                      bias=eps_t[:, 0:1], scale=1.0 / 512))
                            own.settle()
                            act.sem_inc(c_std, 1)
                        if b == 1 and step == 11:
                            act.wait_ge(c_norm, l + 1)
                            for c in range(BC):
                                own.do(act.activation(ys[:, 2, c, :], ys[:, 2, c, :], ACT.Silu,
                                                      bias=p_("ln_c_b")[:, c:c + 1], scale=p_("ln_c_g")[:, c:c + 1]))
                            own.settle()
                            act.sem_inc(src_ready, 1)
                    own.restart()
                for k in range(KC):
                    act.wait_ge(merged_ready, l * KC + (k + 1))
                    own.link(act.copy(a_hi[:, k * T:(k + 1) * T], merged[:, k, :]))
                    act.sem_inc(mhi_ready, 1)
                for k in range(KC):
                    act.wait_ge(prod, l * NM + (M_O + k + 1))
                    split(l, 0, T_O + 4 + k)
                    act.wait_ge(x_mid, l * KC + (k + 1))
                    square(l, 1, k)
                std(l, 1, 1.0 / D)
                modulate(l, 1, lambda k: None)
                own.restart()
                act.wait_ge(keys_in, (l + 1) * 16)

                def take_scores(l, i, s):
                    act.wait_ge(s_prod, l * HP + i * 4 + (s + 1) + 1)
                    act.wait_ge(s_used, l * (HP + 2) + i * 4 + (s + 1))
                    b = 2 * (s % 2)
                    own.do(act.copy(score[:, s % 2, 0:4, :], pm[0:RT_TOK, b, :].rearrange("p (t n) -> p t n", t=4)))
                    own.do(act.copy(score[:, s % 2, 4, :], pm[0:RT_TOK, b + 1, 0:P]))
                    own.settle()
                    act.sem_inc(s_copied, 1)

                with act.Fori(0, HP // 4) as i:
                    for s in range(4):
                        act.wait_ge(s_prod, l * HP + i * 4 + (s - 1 if s >= 1 else 0) + 1)
                        read_product(l, i * 4 + (M_Q + s + 1), s, lambda h, s=s: q_t[:, s % 2, h * HT:(h + 1) * HT], ACT.Copy)
                        act.sem_inc(q_ready, 1)
                        split(l, i, T_Q + 4 + s)
                        if s:
                            take_scores(l, i, s - 1)
                    take_scores(l, i, 3)
                    own.restart()

                def up(l, i, k):
                    s = k % 4
                    act.wait_ge(hid_out[s], (l * (NBLK // 4) + i + k // 4) * 16 + 1)
                    read_product(l, i * 4 + (M_EU + k + 1), k, lambda h, s=s: hid[:, s, h * HT:(h + 1) * HT], ACT.Gelu_apprx_tanh)
                    act.sem_inc(hid_ready, 1)
                    split(l, i, T_EU + 4 + k)

                with act.Fori(0, RT_N) as i:
                    for k in range(12):
                        up(l, i * 3, k)
                        if k == 7:
                            act.wait_ge(e_in, l * RT_N + i + 1)
                            own.link(act.activation(expo[:, :, :], expo[:, :, :], ACT.Exp))
                            act.sem_inc(e_out, 1)
                    act.wait_ge(rt_prod, l * RT_N + i + 1 + 1)
                    own.do(act.copy(rt[:, :, bass.ds(i * RT_TOK, RT_TOK)],
                                    pm[:, 0, 0:3 * RT_TOK].rearrange("p (c t) -> p c t", c=3)))
                    own.settle()
                    act.sem_inc(rt_ready, 1)
                    own.restart()
                own.link(act.copy(g_hi[:, :], rt[:, 2, :]))
                act.sem_inc(ghi_of_picks, 1)
                own.restart()
                with act.Fori(0, GBN) as i:
                    for k in range(4):
                        up(l, i + 3 * RT_N, k)
                        act.wait_ge(g_prod, l * (4 * GBN + 1) + i * 4 + (k + 2) + 1)
                        if k == 0:
                            act.wait_ge(g_out, (l * GBN + i) * 16 + 1)
                        for q, n in ((0, 4), (1, 4), (2, 2)):
                            t0 = k * GS + 4 * q
                            own.do(act.copy(gate_buf[:, :, t0:t0 + n],
                                            pm[:, q, 0:n * P].rearrange("p (t j) -> p j t", t=n)))
                        own.settle()
                        act.sem_inc(g_free, 1)
                    act.sem_inc(passed, 1)
                    act.dma_start(gate_dram[bass.ds(i, 1)].rearrange("o p j t -> p (o j t)"),
                                  gate_buf[:, :, :].rearrange("p j t -> p (j t)")).then_inc(g_out, 16)
                    own.restart()
                with act.Fori(3 * RT_N + GBN, NBLK // 4 - 1) as i:
                    for k in range(4):
                        up(l, i, k)
                    own.restart()

                def gated_hi(l, g, b):
                    act.wait_ge(gated, l * 32 + g + 1)
                    own.link(act.copy(h_hi[:, b], hid_in[:, b]))
                    act.sem_inc(ghi_ready, 1)

                def group(l, i, b):
                    act.wait_ge(prod, l * NM + i * 16 + (M_ED + 8 * b + 1))
                    for s in range(4):
                        split(l, i * 2, T_ED + 4 * (b + 1) + s, odd=b == 0)
                    gated_hi(l, i * 2 + (b + 1), 1 - b)

                gated_hi(l, 0, 0)
                for k in range(4):
                    up(l, NBLK // 4 - 1, k)
                own.restart()
                with act.Fori(0, 15) as i:
                    group(l, i, 0)
                    group(l, i, 1)
                    own.restart()
                group(l, 15, 0)
                own.restart()
            act.wait_ge(x_done, DEPTH + 1)
            for k in range(KC):
                square(DEPTH, 0, k)
            std(DEPTH, 0, 1.0 / D)

        @block.vector
        def _(dve):
            own = Steps(dve, own_dve)
            tt = dve.tensor_tensor

            def split(l, m, s, odd=False):
                dve.wait_ge(hi_ready, l * NT + m + 1)
                tt(ring(False, s, odd), raw[:, s], ring(True, s, odd).bitcast(F32), ALU.subtract).then_inc(lo_ready, 1)

            def take(l, m):
                dve.wait_ge(prod, l * NM + m)

            def release(g):
                own.settle()
                dve.sem_inc(pg_free[g % 2], 1)

            def spread(t, n, size):
                return t.unsqueeze(2).to_broadcast([t.shape[0], t.shape[1], n])

            def norm(l, w, between):
                dve.wait_ge(std_ready, l * 2 + (w + 1))
                own.link(dve.reciprocal(rstd[:, :], rstd[:, :]))
                at = 3 * KC * w
                for k in range(KC):
                    own.link(tt(merged[:, k, :], x[:, k, :], rstd[:, :], ALU.mult))
                    dve.sem_inc(nb_ready, 1)
                own.link(tt(merged[:, :, SEQ:T], merged[:, :, SEQ:T], mod_scale[:, w, :, 1:NC], ALU.mult))
                own.link(tt(merged[:, :, SEQ:T], merged[:, :, SEQ:T], mod[:, at:at + KC, 1:NC], ALU.add))
                dve.sem_inc(nb_ready, 1)
                for k in range(KC):
                    dve.wait_ge(hi_of_nb, l * (2 * KC + 2) + (w * (KC + 1) + k + 1))
                    own.do(tt(a_lo[:, k * T:k * T + SEQ], merged[:, k, 0:SEQ], a_hi[:, k * T:k * T + SEQ].bitcast(F32), ALU.subtract))
                    between(k)
                dve.wait_ge(hi_of_nb, l * (2 * KC + 2) + (w + 1) * (KC + 1))
                own.do(tt(samples(a_lo), merged[:, :, SEQ:T], samples(a_hi).bitcast(F32), ALU.subtract))
                own.settle()
                dve.sem_inc(a_ready, 1)

            def take_ada(l, first, n):
                ada_out = pm[:, 2 if n == ADA_1 else 3, 0:n * NC].rearrange("p (m c) -> p m c", c=NC)
                dve.wait_ge(ada_prod, l * (NMOD // 4) + (first + n) // 4)
                own.link(tt(mod[:, first:first + n, :], ada_out,
                            spread(ada_par[:, bass.ds(l, 1), first:first + n].rearrange("p o m -> p (o m)"), NC, n), ALU.add))
                dve.sem_inc(mod_taken, 1)

            def scale_of(l, w):
                at = KC + 3 * KC * w
                own.link(dve.tensor_scalar(mod_scale[:, w], mod[:, at:at + KC, :], 1.0, None, ALU.add))
                g = ada_par[:, bass.ds(l, 1), NMOD + w * KC:NMOD + (w + 1) * KC].rearrange("p o m -> p (o m)")
                own.link(tt(mod_scale[:, w], mod_scale[:, w], spread(g, NC, KC), ALU.mult))

            dve.wait_ge(consts, 1)
            dve.wait_ge(x_in, 64)
            with dve.Fori(0, DEPTH) as l:
                dve.wait_ge(x_done, l + 1)
                take_ada(l, 0, ADA_1)
                scale_of(l, 0)
                dve.wait_ge(par_in, (l + 1) * (16 * (1 + 2 * BC)))
                norm(l, 0, lambda k: split(l, k // 2, k // 2) if k % 2 else None)
                own.restart()
                for t in range(5):
                    dve.wait_ge(v_gelu, l * 5 + (t + 1))
                    own.link(dve.bn_stats(v_stat[:, t, :], v_tok[:, t, :]))
                    own.link(dve.bn_aggr(v_mv[:, t, :], v_stat[:, t, :]))
                dve.sem_inc(v_stats, 1)
                for s in range(4):
                    split(l, 4 + s, s)
                dve.wait_ge(v_std, l + 1)
                own.link(dve.reciprocal(v_rstd[:, :], v_rstd[:, :]))
                for c in range(BC):
                    if c == 1:
                        take_ada(l, ADA_1, 4)
                    for t in ((0, 1), (2, 3), (4,), ())[c]:
                        own.do(dve.tensor_scalar(v_tok[:, t, :], v_tok[:, t, :], v_mv[:, t, 0:1], v_rstd[:, t:t + 1],
                                                 ALU.subtract, ALU.mult))
                    own.settle()
                    if c >= 2:
                        wide = p_(("ln_a_g", "ln_a_b")[c - 2]).unsqueeze(1).to_broadcast([P, 5, 512])
                        own.link(tt(v_tok[:, :, :], v_tok[:, :, :], wide, (ALU.mult, ALU.add)[c - 2]))
                    split(l, T_B + c, c)
                dve.sem_inc(v_ready, 1)

                def times_factor(l, n, c, wide, narrow, w, count):
                    dve.wait_ge(fac_ready, l * 8 + (count + 1))
                    take(l, n + 1)
                    g = n % 2
                    own.do(tt(wide[:, c, w - 1:w - 1 + HT], pg[:, g, 0, 0:HT], fac[:, c % 2, 0:HT], ALU.mult))
                    own.do(tt(wide[:, c, w - 1 + HT:w - 1 + SEQ], pg[:, g, 1, 0:H1P], fac[:, c % 2, HT:SEQ], ALU.mult))
                    own.do(tt(narrow[:, c, :, w - 1], pg[:, g, 1, H1P:HT], fac[:, c % 2, SEQ:T], ALU.mult))
                    release(g)
                    dve.sem_inc(fac_used, 1)

                dve.wait_ge(trunk_init, l + 1)
                for c in range(BC):
                    n = T_B + 2 * c
                    split(l, n + 4, 0 if c % 2 == 0 else 2)
                    times_factor(l, n + 1, c, cin, cin_s, WB, c)
                    if c % 2 == 0:
                        take_ada(l, ADA_1 + 4 + 2 * c, 4)
                    split(l, n + 5, 1 if c % 2 == 0 else 3)
                dve.sem_inc(cin_ready, 1)

                w_b = p_("conv_b").rearrange("p (c w) -> p c w", c=BC)

                def conv_b(c):
                    own.link(dve.tensor_scalar(ys[:, 0, c, 0:SEQ], cin[:, c, 0:SEQ], w_b[:, c, 0:1], None, ALU.mult))
                    for k in range(1, WB):
                        own.link(dve.scalar_tensor_tensor(out=ys[:, 0, c, 0:SEQ], in0=cin[:, c, k:k + SEQ], scalar=w_b[:, c, k:k + 1],
                                                          in1=ys[:, 0, c, 0:SEQ], op0=ALU.mult, op1=ALU.add))

                def conv_b_samples():
                    for c in range(BC):
                        own.do(tt(prod_s[:, c], cin_s[:, c], w_b[:, c, :].unsqueeze(1).to_broadcast([P, NS, WB]), ALU.mult))
                    own.settle()
                    for c in range(BC):
                        own.do(dve.tensor_reduce(ys[:, 0, c, SEQ:T], prod_s[:, c], AX_X, ALU.add))
                    own.settle()

                def mix(l, g, first):
                    dve.wait_ge(mix_prod, l * BC + (first + 1))
                    own.link(tt(mix_t[:, :].rearrange("p (c t) -> p c t", c=4), pm[:, g, :].rearrange("p (c t) -> p c t", c=4),
                                p_("b_s")[:, g * P:(g + 1) * P].unsqueeze(1).to_broadcast([P, 4, P]), ALU.add))
                    own.do(tt(ys[:, 1, g, 0:SEQ], mix_t[:, :], ys[:, 1, g, 0:SEQ], ALU.mult))
                    own.do(dve.tensor_scalar(tmp8[:, :], vs_t[:, g, :], p_("w_s00")[:, g:g + 1], p_("b_s")[:, g * P:g * P + 1],
                                             ALU.mult, ALU.add))
                    own.settle()
                    own.link(tt(ys[:, 1, g, SEQ:T], ys[:, 1, g, SEQ:T], tmp8[:, :], ALU.mult))

                dve.wait_ge(u_ready, l + 1)
                for c in range(BC):
                    n = T_C + 2 * c
                    split(l, n + 4, 0 if c % 2 == 0 else 2)
                    conv_b(c)
                    times_factor(l, n + 1, c, glu, glu_s, WC, 4 + c)
                    split(l, n + 5, 1 if c % 2 == 0 else 3)
                    if c == 1:
                        dve.wait_ge(vt_ready, l + 1)
                    if c >= 1:
                        mix(l, c, c - 1)
                    else:
                        conv_b_samples()
                dve.sem_inc(glu_ready, 1)
                mix(l, 0, 3)

                w_c = p_("conv_c").rearrange("p (c w) -> p c w", c=BC)
                taps = [(c, k) for c in range(BC - 1) for k in range(WC)]

                def conv_c(n):
                    for c, k in [taps.pop(0) for _ in range(min(n, len(taps)))]:
                        if k == 0:
                            own.link(dve.tensor_scalar(ys[:, 2, c, 0:SEQ], glu[:, c, 0:SEQ], w_c[:, c, 0:1],
                                                       p_("conv_c_b")[:, c:c + 1], ALU.mult, ALU.add))
                        else:
                            own.link(dve.scalar_tensor_tensor(out=ys[:, 2, c, 0:SEQ], in0=glu[:, c, k:k + SEQ], scalar=w_c[:, c, k:k + 1],
                                                              in1=ys[:, 2, c, 0:SEQ], op0=ALU.mult, op1=ALU.add))

                def conv_c_samples(c):
                    own.link(tt(prod_c[:, :, :], glu_s[:, c], w_c[:, c, :].unsqueeze(1).to_broadcast([P, NS, WC]), ALU.mult))
                    own.link(dve.tensor_reduce(tmp8[:, :], prod_c[:, :, :], AX_X, ALU.add))
                    own.link(dve.tensor_scalar(ys[:, 2, c, SEQ:T], tmp8[:, :], p_("conv_c_b")[:, c:c + 1], None, ALU.add))

                for c in range(BC):
                    take(l, T_BB + c + 1)
                    if c == 1:
                        take_ada(l, ADA_1 + 12, 4)
                    for h in range(2):
                        s_ = slice(h * HT, (h + 1) * HT)
                        own.do(tt(ys[:, 0, c, s_], pg[:, c % 2, h, 0:HT], ys[:, 0, c, s_], ALU.mult))
                    release(c)
                    split(l, T_BB + 4 + c, c)
                    conv_c(3)
                dve.sem_inc(src_ready, 2)
                own.restart()

                def centre_c():
                    dve.wait_ge(c_sum, l + 1)
                    for h in range(2):
                        own.do(dve.tensor_scalar(mean[:, h * HT:(h + 1) * HT], pm[:, h, 0:HT], 1.0 / 512, None, ALU.mult))
                    own.settle()
                    for c in range(BC):
                        own.do(tt(ys[:, 2, c, :], ys[:, 2, c, :], mean[:, :], ALU.subtract))
                    own.settle()
                    dve.sem_inc(c_cent, 1)

                def normalise_c():
                    dve.wait_ge(c_std, l + 1)
                    own.link(dve.reciprocal(rstd[:, :], rstd[:, :]))
                    for c in range(BC):
                        own.do(tt(ys[:, 2, c, :], ys[:, 2, c, :], rstd[:, :], ALU.mult))
                    own.settle()
                    dve.sem_inc(c_norm, 1)

                dve.wait_ge(early_out, (l + 1) * (16 * (2 + BC)))
                for b in range(3):
                    for step in range(12):
                        n = T_BR + 12 * b + step
                        if not (step < 4 or 6 <= step < 10):
                            q = (step - 4) if step < 6 else step - 8
                            for d in (2 * q, 2 * q + 1):
                                m = M_BR + 16 * b + (4 + d if d < 4 else 8 + d)
                                dve.wait_ge(sig_ready, l * 24 + (8 * b + d + 1))
                                take(l, m + 1)
                                for h in range(2):
                                    s_ = slice(h * HT, (h + 1) * HT)
                                    own.do(tt(merged[:, d, s_] if b == 0 else sig[:, d % 4, s_], pg[:, m % 2, h, 0:HT],
                                              sig[:, d % 4, s_], ALU.mult))
                                release(m)
                                if b:
                                    own.link(tt(merged[:, d, :], merged[:, d, :], sig[:, d % 4, :], ALU.add))
                                dve.sem_inc(sig_used, 1)
                                if b == 2:
                                    dve.sem_inc(merged_ready, 1)
                        split(l, n + 4, step % 4)
                        if step % 4 == 1 and (b == 0 or b == 1 and step == 1):
                            take_ada(l, ADA_1 + 16 + 12 * b + step - 1, 4)
                        if step == 2:
                            dve.wait_ge(yhi_ready, l * 3 + (b + 1))
                            own.link(tt(y_lo[:, :, :], ys[:, b, :, :], y_hi[:, :, :].bitcast(F32), ALU.subtract))
                            dve.sem_inc(y_ready, 1)
                        if b == 0 or b == 1 and step < 4:
                            conv_c(5 + (step % 2))
                        if b == 1 and step == 4:
                            conv_c(99)
                            for c in range(BC):
                                conv_c_samples(c)
                            dve.wait_ge(conv_pool, l + 1)
                            dve.sem_inc(conv_ready, 1)
                        if b == 1 and step == 7:
                            centre_c()
                        if b == 1 and step == 11:
                            normalise_c()
                    own.restart()
                for k in range(KC):
                    dve.wait_ge(mhi_ready, l * KC + (k + 1))
                    own.link(tt(a_lo[:, k * T:(k + 1) * T], merged[:, k, :], a_hi[:, k * T:(k + 1) * T].bitcast(F32), ALU.subtract))
                dve.sem_inc(merged_split, 1)
                own.restart()

                for k in range(KC):
                    gate = mod[:, 2 * KC + k, :]
                    take(l, M_O + k + 1)
                    own.do(tt(tmp8[:, :], pg[:, k % 2, 1, H1P:HT], gate[:, 1:NC], ALU.mult))
                    for h, a, b_, ta, tb in PARTS:
                        own.do(dve.scalar_tensor_tensor(out=x[:, k, ta:tb], in0=pg[:, k % 2, h, a:b_], scalar=gate[:, 0:1],
                                                        in1=x[:, k, ta:tb], op0=ALU.mult, op1=ALU.add))
                    own.settle()
                    own.link(tt(x[:, k, SEQ:T], x[:, k, SEQ:T], tmp8[:, :], ALU.add))
                    release(k)
                    dve.sem_inc(x_mid, 1)
                    split(l, T_O + 4 + k, k % 4)
                own.restart()
                scale_of(l, 1)
                norm(l, 1, lambda k: None)
                own.restart()

                def tops_of(l, i, s):
                    dve.wait_ge(s_copied, l * HP + i * 4 + (s + 1) + 1)
                    dve.sem_inc(passed, 1)
                    sc = score[:, s % 2]
                    for t in range(RT_N):
                        own.do(dve.max(pick_v[:, s, t, 0:8], sc[:, t, :]))
                    own.settle()
                    for t in range(RT_N):
                        own.do(dve.max_index(pick_i[:, s, t, 0:8], pick_v[:, s, t, 0:8], sc[:, t, :]))
                        own.do(dve.match_replace(score_r[:, t, :], pick_v[:, s, t, 0:8], sc[:, t, :], NEG))
                    own.settle()
                    dve.sem_inc(s_used, 1)
                    for t in range(RT_N):
                        own.do(dve.max(pick_v[:, s, t, 8:16], score_r[:, t, :]))
                    own.settle()
                    for t in range(RT_N):
                        own.do(dve.max_index(pick_i[:, s, t, 8:16], pick_v[:, s, t, 8:16], score_r[:, t, :]))
                    own.settle()

                dve.sem_inc(s_used, 2)
                with dve.Fori(0, HP // 4) as i:
                    for s in range(4):
                        split(l, i * 4 + (T_Q + 4 + s), s)
                        if s:
                            tops_of(l, i, s - 1)
                    tops_of(l, i, 3)
                    for s in range(4):
                        own.do(dve.tensor_copy(top_v[:, :, bass.ds(i * 4 + s, 1), :].rearrange("p t o k -> p t (o k)"), pick_v[:, s]))
                        own.do(dve.tensor_copy(top_i[:, :, bass.ds(i * 4 + s, 1), :].rearrange("p t o k -> p t (o k)"), pick_i[:, s]))
                    own.settle()
                    own.restart()

                dve.wait_ge(rt_ready, l * RT_N + 1)
                dve.sem_inc(passed, 1)
                iota16 = iota_f[0:RT_TOK, 0:TOPK].unsqueeze(1).to_broadcast([RT_TOK, P, TOPK])

                def of_tile(t, i):
                    return t[:, bass.ds(i, 1)].rearrange("p o (h z) k -> p (o h) z k", z=2)

                def each_head(f):
                    for h in range(HEADS):
                        own.do(f(h))
                    own.settle()

                def route_piece(l, i, k):
                    shape = [RT_TOK, HEADS, TOPK, TOPK]
                    if k == 0:
                        v = of_tile(top_v, i)
                        own.link(tt(cand[:, :, :].rearrange("p h (a b) -> p h a b", a=TOPK),
                                    v[:, :, 0, :].unsqueeze(3).to_broadcast(shape), v[:, :, 1, :].unsqueeze(2).to_broadcast(shape), ALU.add))
                    if k == 1:
                        each_head(lambda h: dve.max(best[:, h, 0:8], cand[:, h, :]))
                    if k == 2:
                        each_head(lambda h: dve.max_index(pos[:, h * TOPK:h * TOPK + 8], best[:, h, 0:8], cand[:, h, :]))
                    if k == 3:
                        each_head(lambda h: dve.match_replace(cand_r[:, h, :], best[:, h, 0:8], cand[:, h, :], NEG))
                    if k == 4:
                        each_head(lambda h: dve.max(best[:, h, 8:16], cand_r[:, h, :]))
                    if k == 5:
                        own.link(tt(expo[:, :, :], best[:, :, :], best[:, :, 0:1].to_broadcast([RT_TOK, HEADS, TOPK]), ALU.subtract))
                        dve.sem_inc(e_in, 1)
                        each_head(lambda h: dve.max_index(pos[:, h * TOPK + 8:h * TOPK + 16], best[:, h, 8:16], cand_r[:, h, :]))
                    if k == 6:
                        own.do(dve.tensor_scalar(pos_h[:, 0], pos[:, :], 4, None, ALU.logical_shift_right))
                        own.do(dve.tensor_scalar(pos_h[:, 1], pos[:, :], 15, None, ALU.bitwise_and))
                        own.settle()
                        own.link(dve.tensor_copy(pos_f[:, :, :], pos_h[:, :, :]))
                    if k in (7, 9):
                        z = (k - 7) // 2
                        own.link(tt(eq[:, :, :], iota16, pos_f[:, z, :].unsqueeze(2).to_broadcast([RT_TOK, P, TOPK]), ALU.is_equal))
                    if k in (8, 10):
                        z = (k - 8) // 2
                        dve.wait_ge(rt_prod, l * RT_N + i + 1)
                        e4 = eq[:, :, :].rearrange("p (h k) a -> p h k a", h=HEADS)
                        own.link(tt(e4, e4, of_tile(top_i, i)[:, :, z, :].unsqueeze(2).to_broadcast(shape), ALU.mult))
                        own.link(dve.tensor_reduce(picked[:, z, :], eq[:, :, :], AX_X, ALU.add))
                    if k == 11:
                        dve.wait_ge(e_out, l * RT_N + i + 1)
                        own.link(dve.tensor_reduce(esum[:, :], expo[:, :, :], AX_X, ALU.add))
                        own.link(dve.reciprocal(esum[:, :], esum[:, :]))
                        own.link(tt(picked[:, 2, :].rearrange("p (h k) -> p h k", h=HEADS), expo[:, :, :],
                                    esum[:, :].unsqueeze(2).to_broadcast([RT_TOK, HEADS, TOPK]), ALU.mult))
                        dve.sem_inc(picks_ready, 1)

                with dve.Fori(0, RT_N) as i:
                    for k in range(12):
                        route_piece(l, i, k)
                        split(l, i * 12 + (T_EU + 4 + k), k % 4)
                    own.restart()

                iota_b = iota_f[:, :].unsqueeze(1).to_broadcast([P, GS, P])
                dve.wait_ge(rt_ready, (l + 1) * RT_N + 1)
                dve.wait_ge(ghi_of_picks, l + 1)
                own.link(tt(g_lo[:, :], rt[:, 2, :], g_hi[:, :].bitcast(F32), ALU.subtract))
                dve.sem_inc(eq_ready, 1)
                own.restart()
                dve.sem_inc(passed, 1)
                dve.sem_inc(g_prod, 1)

                def one_hots(l, i, k):
                    def of(t, c):
                        return t[:, c, bass.ds(i * GB + k * GS, GS)].unsqueeze(2).to_broadcast([P, GS, P])
                    dve.wait_ge(g_prod, l * (4 * GBN + 1) + i * 4 + k + 1)
                    own.do(tt(one_i[:, k % 2], iota_b, of(rt, 0), ALU.is_equal))
                    own.do(tt(eq_j[:, k % 2], iota_b, of(rt, 1), ALU.is_equal))
                    own.settle()
                    dve.sem_inc(eq_ready, 1)
                    own.link(tt(one_j[:, k % 2, 0], eq_j[:, k % 2], of(g_hi[:, :].bitcast(F32).unsqueeze(1), 0), ALU.mult))
                    dve.sem_inc(one_ready, 1)

                one_hots(l, 0, 0)
                own.restart()
                with dve.Fori(0, GBN - 1) as i:
                    for k in range(4):
                        one_hots(l, i, k + 1)
                        split(l, i * 4 + (T_EU + 12 * RT_N + 4 + k), k)
                    own.restart()
                for k in range(4):
                    if k < 3:
                        one_hots(l, GBN - 1, k + 1)
                    split(l, T_EU + 12 * RT_N + 4 * GBN + k, k)
                own.restart()
                with dve.Fori(T_EU // 4 + 3 * RT_N + GBN, T_ED // 4 - 1) as i:
                    for k in range(4):
                        split(l, i * 4 + (4 + k), k)

                def gate_times_hidden(l, i, b):
                    dve.wait_ge(down_in[b], (l * 16 + i + 1) * 32)
                    own.link(tt(hid_in[:, b].rearrange("p j (b t) -> p j b t", t=GB), hid_in[:, b].rearrange("p j (b t) -> p j b t", t=GB),
                                gate_in[:, b].rearrange("p b (j t) -> p j b t", t=GB), ALU.mult))
                    dve.sem_inc(gated, 1)

                def gated_lo(l, g, b):
                    dve.wait_ge(ghi_ready, l * 32 + g + 1)
                    own.link(tt(h_lo[:, b], hid_in[:, b], h_hi[:, b].bitcast(F32), ALU.subtract))
                    dve.sem_inc(g_ready, 1)

                def group(l, i, b, last=False):
                    for d in range(KC):
                        take(l, i * 16 + (M_ED + 8 * b + d + 1))
                        for h in range(2):
                            s_ = slice(h * HT, (h + 1) * HT)
                            own.do(tt(acc[:, d, s_], acc[:, d, s_], pg[:, d % 2, h, 0:HT], ALU.add))
                        release(d)
                        if last:
                            continue
                        if d == 0:
                            gate_times_hidden(l, i + b, 1 - b)
                        if 1 <= d <= 4:
                            split(l, i * 8 + (T_ED + 4 * (b + 1) + d - 1), d - 1, odd=b == 0)
                        if d == 5:
                            gated_lo(l, i * 2 + (b + 1), 1 - b)

                gate_times_hidden(l, 0, 0)
                gated_lo(l, 0, 0)
                for k in range(4):
                    split(l, T_ED + k, k)
                dve.wait_ge(acc_zero, l + 1)
                dve.sem_inc(passed, 1)
                own.restart()
                with dve.Fori(0, 15) as i:
                    group(l, i, 0)
                    group(l, i, 1)
                    own.restart()
                group(l, 15, 0)
                group(l, 15, 1, last=True)
                for k in range(KC):
                    gate = mod[:, 5 * KC + k, :]
                    own.do(dve.scalar_tensor_tensor(out=x[:, k, 0:SEQ], in0=acc[:, k, 0:SEQ], scalar=gate[:, 0:1],
                                                    in1=x[:, k, 0:SEQ], op0=ALU.mult, op1=ALU.add))
                    own.link(tt(acc[:, k, SEQ:T], acc[:, k, SEQ:T], gate[:, 1:NC], ALU.mult))
                    own.link(tt(x[:, k, SEQ:T], x[:, k, SEQ:T], acc[:, k, SEQ:T], ALU.add))
                dve.sem_inc(x_done, 1)
                own.restart()
            dve.wait_ge(std_ready, 2 * DEPTH + 1)
            own.link(dve.reciprocal(rstd[:, :], rstd[:, :]))
            for k in range(KC):
                own.link(dve.scalar_tensor_tensor(out=x[:, k, :], in0=x[:, k, :], scalar=fin_g[:, k:k + 1], in1=rstd[:, :],
                                                  op0=ALU.mult, op1=ALU.mult))
                dve.sem_inc(y_fin, 1)

        @block.tensor
        def _(pe):
            def both(outs, w, a, first, last):
                for h in range(2):
                    pe.matmul(outs[h], w[0], a[h][0], start=first, stop=False)
                    pe.matmul(outs[h], w[0], a[h][1], start=False, stop=False)
                for h in range(2):
                    mm = pe.matmul(outs[h], w[1], a[h][0], start=False, stop=last)
                return mm

            def weights(l, m):
                pe.wait_ge(lo_ready, l * NT + m + 1 + 1)

            def buffer(l, g, parity):
                pe.wait_ge(pg_free[parity], l * NG + g + 1)

            def chunk(k, h):
                return act_chunk(a_hi, k, h), act_chunk(a_lo, k, h)

            def product(parity, s, rhs, ks=range(KC)):
                outs = [pg[:, parity, h, 0:HT] for h in range(2)]
                for n, k in enumerate(ks):
                    mm = both(outs, (w_hi[:, s, k, :], w_lo[:, s, k, :]), [rhs(n, h) for h in range(2)], n == 0, n == len(ks) - 1)
                mm.then_inc(prod, 1)

            def square_sum(l, base, k):
                pe.wait_ge(sq_ready, l * (2 * KC) + (base * KC + k + 1))
                for h in range(2):
                    mm = pe.matmul(pm[:, h, 0:HT], ones[:, :], sq[:, k % 2, h * HT:(h + 1) * HT], start=k == 0, stop=k == KC - 1)
                mm.then_inc(sq_used, 1)

            def ada(l, turn):
                for s in range(4):
                    pe.wait_ge(raw_in[s], (l * RAW_PER_SLOT + turn) * 16)
                for k in range(KC):
                    mm = pe.matmul(pm[0:NC, 3, :], cond_silu[:, k, :], raw[:, :, k, :], start=k == 0, stop=k == KC - 1)
                mm.then_inc(ada_done, 1)

            def ada_turn(l, n, bank, at):
                pe.wait_ge(ada_row_ready, l * (NMOD // 4) + n + 1)
                pe.sem_inc(passed, 1)
                for s in range(4):
                    mm = pe.transpose(pm[:, bank, at + s * NC:at + (s + 1) * NC], ada_row[:, s * P:(s + 1) * P], ident[0:NC, 0:NC])
                mm.then_inc(ada_prod, 1)

            def ada_batch(l, i, late):
                pe.wait_ge(mod_taken, l * (1 + len(ADA_AT)) + i + (1 - 2 * late))
                ada(l, i * 2 + (ADA_1 // 4 + 1 - 2 * late))

            pe.wait_ge(consts, 1)
            pe.wait_ge(silu_ready, 1)
            with pe.Fori(0, DEPTH) as l:
                pe.wait_ge(mod_taken, l * (1 + len(ADA_AT)) + 1)
                for n in range(ADA_1 // 4):
                    ada(l, n + 1)
                    square_sum(l, 0, 2 * n)
                    square_sum(l, 0, 2 * n + 1)
                    ada_turn(l, n, 2, n * 4 * NC)
                pe.wait_ge(a_ready, l * 2 + 1)
                weights(l, 3)
                for t in range(5):
                    t0 = t * P if t < 4 else T - P
                    if t == 4:
                        pe.wait_ge(v_gelu, l * 5 + 1)
                    for k in range(KC):
                        tok = slice(k * T + t0, k * T + t0 + P)
                        hi, lo = w_hi[:, :, k, :], w_lo[:, :, k, :]
                        out = pm[:, t % 4, :]
                        pe.matmul(out, a_hi[:, tok], hi, start=k == 0, stop=False)
                        pe.matmul(out, a_hi[:, tok], lo, start=False, stop=False)
                        mm = pe.matmul(out, a_lo[:, tok], hi, start=False, stop=k == KC - 1)
                    if t < 4:
                        mm.then_inc(v_prod, 1)
                    else:
                        mm.then_inc(prod, 4)
                pe.wait_ge(v_gelu, l * 5 + 4)
                pe.sem_inc(passed, 1)
                with pe.Fori(1, 4) as i:
                    for s in range(4):
                        weights(l, i * 4 + s)
                        buffer(l, i * 2 + (s // 2 - 2), s % 2)
                        product(s % 2, s, chunk)
                        if s == 0:
                            ada_batch(l, i, 0)
                        if s == 1:
                            ada_turn(l, i + 3, 3, 0)
                pe.wait_ge(v_ready, l + 1)
                pe.wait_ge(mask_done, l + 1)
                pe.wait_ge(mod_taken, l * (1 + len(ADA_AT)) + 5)
                for g in range(BC):
                    mm = pe.transpose(pm[:, 0, g * P:(g + 1) * P], v_tok[:, 4, g * P:(g + 1) * P], ident[:, :])
                mm.then_inc(vt_prod, 1)
                for g in (1, 2, 3):
                    for c in range(4):
                        mm = pe.matmul(pm[:, g, c * P:(c + 1) * P], v_tok[:, c, g * P:(g + 1) * P],
                                       p_("w_s")[:, g * P:(g + 1) * P], start=True, stop=True)
                    mm.then_inc(mix_prod, 1)
                with pe.Fori(4, 6) as i:
                    for s in range(4):
                        weights(l, i * 4 + s)
                        buffer(l, i * 2 + (s // 2 - 2), s % 2)
                        product(s % 2, s, chunk)
                pe.wait_ge(vt_ready, l + 1)
                for c in range(4):
                    mm = pe.matmul(pm[:, 0, c * P:(c + 1) * P], v_tok[:, c, 0:P], p_("w_s")[:, 0:P], start=True, stop=True)
                mm.then_inc(mix_prod, 1)
                pe.wait_ge(glu_ready, l + 1)
                for s in range(4):
                    weights(l, T_BB + s)
                    buffer(l, (T_BB - 4 + s) // 2, s % 2)
                    product(s % 2, s, chunk)
                    if s == 0:
                        ada_batch(l, T_BB // 4, 1)
                    if s == 1:
                        ada_turn(l, 7, 3, 0)
                for b in range(3):
                    for step in range(12):
                        s = step % 4
                        weights(l, T_BR + 12 * b + step)
                        if step < 4 or 6 <= step < 10:
                            d = step if step < 4 else step - 2
                            g = G_BR + 16 * b + (d if d < 4 else d + 4)
                            buffer(l, g // 2, g % 2)
                            product(g % 2, s, chunk)
                        else:
                            q = (step - 4) if step < 6 else step - 8
                            if q == 0:
                                pe.wait_ge(y_ready, l * 3 + (b + 1))
                            for e in range(2):
                                d = 2 * q + e
                                g = G_BR + 16 * b + (4 + d if d < 4 else 8 + d)
                                buffer(l, g // 2, g % 2)
                                product(g % 2, s, lambda n, h: (y_hi[:, n, h * HT:(h + 1) * HT], y_lo[:, n, h * HT:(h + 1) * HT]),
                                        range(4 * e, 4 * e + 4))
                        if b == 0 or b == 1 and step < 4:
                            if step % 4 == 0:
                                ada_batch(l, (T_BR + 12 * b + step) // 4, 1)
                            if step % 4 == 1:
                                ada_turn(l, 8 + 3 * b + step // 4, 3, 0)
                        if b == 1 and step == 6:
                            pe.wait_ge(conv_ready, l + 1)
                            for c in range(BC):
                                for h in range(2):
                                    mm = pe.matmul(pm[:, h, 0:HT], ones[:, :], ys[:, 2, c, h * HT:(h + 1) * HT], start=c == 0, stop=c == BC - 1)
                            mm.then_inc(c_sum, 1)
                        if b == 1 and step == 9:
                            for c in range(BC):
                                pe.wait_ge(c_sq, l * BC + (c + 1))
                                for h in range(2):
                                    mm = pe.matmul(pm[:, 2 + h, 0:HT], ones[:, :], sq[:, c % 2, h * HT:(h + 1) * HT], start=c == 0, stop=c == BC - 1)
                                mm.then_inc(c_sqsum, 1)
                pe.wait_ge(merged_split, l + 1)
                for k in range(KC):
                    weights(l, T_O + k)
                    buffer(l, G_O // 2 + k // 2, k % 2)
                    product(k % 2, k % 4, chunk)
                    if k >= 2:
                        square_sum(l, 1, k - 2)
                for k in range(KC - 2, KC):
                    square_sum(l, 1, k)
                pe.wait_ge(a_ready, l * 2 + 2)
                pe.sem_inc(passed, 1)

                def scores(l, i, s):
                    pe.wait_ge(keys_in, (l + 1) * 16)
                    pe.wait_ge(q_ready, l * HP + i * 4 + (s + 1))
                    pe.wait_ge(s_copied, l * HP + i * 4 + (s - 1 if s >= 1 else 0) + 1)
                    for t in range(RT_N):
                        b, c = 2 * (s % 2) + t // 4, (t % 4) * P
                        mm = pe.matmul(pm[0:RT_TOK, b, c:c + P], q_t[:, s % 2, t * RT_TOK:(t + 1) * RT_TOK],
                                       keys[:, bass.ds(i * 4 + s, 1), :].rearrange("p o n -> p (o n)"), start=True, stop=True)
                    mm.then_inc(s_prod, 1)

                with pe.Fori(0, HP // 4) as i:
                    for s in range(4):
                        weights(l, i * 4 + (T_Q + s))
                        buffer(l, i * 2 + (G_Q // 2 + s // 2), s % 2)
                        product(s % 2, s, chunk)
                        if s:
                            scores(l, i, s - 1)
                    scores(l, i, 3)

                def up(l, i, k):
                    weights(l, i * 4 + (T_EU + k))
                    buffer(l, i * 2 + (G_EU // 2 + k // 2), k % 2)
                    product(k % 2, k % 4, chunk)

                with pe.Fori(0, RT_N) as i:
                    for k in range(12):
                        up(l, i * 3, k)
                    pe.wait_ge(picks_ready, l * RT_N + i + 1)
                    pe.wait_ge(rt_ready, l * RT_N + i + 1)
                    for c in range(3):
                        mm = pe.transpose(pm[:, 0, c * RT_TOK:(c + 1) * RT_TOK], picked[:, c, :], ident[0:RT_TOK, 0:RT_TOK])
                    mm.then_inc(rt_prod, 1)
                pe.wait_ge(rt_ready, (l + 1) * RT_N + 1)
                pe.sem_inc(passed, 1)
                with pe.Fori(0, GBN) as i:
                    for k in range(4):
                        up(l, i + 3 * RT_N, k)
                        pe.wait_ge(one_ready, l * (4 * GBN) + i * 4 + (k + 1))
                        pe.wait_ge(one_lo_ready, l * (4 * GBN) + i * 4 + (k + 1))
                        pe.wait_ge(g_free, l * (4 * GBN) + i * 4 + k + 1)
                        for t in range(GS):
                            for z in range(2):
                                mm = pe.matmul(pm[:, t // 4, (t % 4) * P:(t % 4 + 1) * P], one_i[:, k % 2, t, :],
                                               one_j[:, k % 2, z, t, :], start=z == 0, stop=z == 1)
                        mm.then_inc(g_prod, 1)
                with pe.Fori(3 * RT_N + GBN, NBLK // 4) as i:
                    for k in range(4):
                        up(l, i, k)

                def group(l, i, b):
                    weights(l, i * 8 + (T_ED + 4 * b + 3))
                    pe.wait_ge(g_ready, l * 32 + i * 2 + (b + 1))
                    for d in range(KC):
                        buffer(l, i * 8 + (G_ED // 2 + 4 * b + d // 2), d % 2)
                        outs = [pg[:, d % 2, h, 0:HT] for h in range(2)]
                        for j in range(4):
                            w = ring(True, j, b == 1)[:, d, :], ring(False, j, b == 1)[:, d, :]
                            a = [(h_hi[:, b, j, h * HT:(h + 1) * HT], h_lo[:, b, j, h * HT:(h + 1) * HT]) for h in range(2)]
                            mm = both(outs, w, a, j == 0, j == 3)
                        mm.then_inc(prod, 1)

                with pe.Fori(0, 16) as i:
                    group(l, i, 0)
                    group(l, i, 1)
            pe.wait_ge(x_done, DEPTH + 1)
            for k in range(KC):
                square_sum(DEPTH, 0, k)


def _lay_out(i, np):
    L = DEPTH

    def tiles(w):
        k, m = w.shape
        return w.reshape(k // P, P, m // P, P).transpose(2, 1, 0, 3)

    def channels(a):
        return np.moveaxis(a.reshape(*a.shape[:-1], -1, P), (-1, -2), (0, 1))

    def wide(a):
        return np.broadcast_to(a.reshape(1, -1), (P, a.size))

    stream = np.empty((L, NMOD + NT, P, KC, P), np.float32)
    params = np.empty((L, P, NPAR), np.float32)
    for l in range(L):
        s = stream[l]
        s[0:NMOD] = tiles(i["ada_w"][l])
        t = s[NMOD:]
        w_in = tiles(i["w_in"][l])
        u, v, hb, bb, cb, ac, gc = (w_in[4 * n:4 * n + 4] for n in range(7))
        t[T_V:T_V + 4], t[T_U:T_U + 4] = v, u
        t[T_B:T_C:2], t[T_B + 1:T_C:2] = hb, cb
        t[T_C:T_BB:2], t[T_C + 1:T_BB:2] = gc, ac
        t[T_BB:T_BR] = bb
        for b, r in enumerate((1, 0, 2)):
            n = T_BR + 12 * b
            gates = w_in[28 + 8 * r:36 + 8 * r]
            br = tiles(i["w_branch"][l, r]).reshape(4, 2, P, BC, P).transpose(0, 2, 1, 3, 4).reshape(4, P, KC, P)
            t[n:n + 4], t[n + 4:n + 6], t[n + 6:n + 10], t[n + 10:n + 12] = gates[0:4], br[0:2], gates[4:8], br[2:4]
        t[T_O:T_Q] = tiles(i["w_out"][l])
        t[T_Q:T_EU] = tiles(i["peer_w_query"][l])
        t[T_EU:T_ED] = i["peer_u"][l].reshape(P, NBLK, KC, P).transpose(1, 3, 2, 0)
        t[T_ED:NT] = i["peer_v"][l].reshape(P, NBLK, KC, P).transpose(1, 0, 2, 3)

        def put(name, a):
            params[l][:, PAR[name][0]:PAR[name][1]] = a.reshape(P, -1)

        put("ln_a_g", wide(i["ln_a_g"][l]))
        put("ln_a_b", wide(i["ln_a_b"][l]))
        put("w_s", i["w_spatial"][l].transpose(2, 0, 1))
        put("b_s", wide(i["b_spatial"][l]))
        put("w_s00", wide(i["w_spatial"][l, :, 0, 0]))
        put("conv_b", channels(i["conv_b_w"][l]))
        put("conv_c", channels(i["conv_c_w"][l]))
        for name, key in (("conv_c_b", "conv_c_b"), ("ln_c_g", "ln_c_g"), ("ln_c_b", "ln_c_b")):
            put(name, channels(i[key][l]))
    tokens = np.concatenate([i["x_prompt"].reshape(SEQ, D), i["x_sample"].reshape(NS, D)])
    cond = np.concatenate([i["c_prompt"], i["c_sample"]])

    def history(a):
        l, s, w, c = a.shape
        return a.reshape(l, s, w, c // P, P).transpose(0, 4, 3, 1, 2)

    return {
        "stream": stream, "x_t": channels(tokens), "c_t": channels(cond), "final_g": channels(i["final_g"]),
        "ada_params": np.concatenate([channels(i["ada_b"]).transpose(0, 2, 1),
                                      channels(i["norm_g"]).transpose(0, 2, 3, 1).reshape(P, L, 2 * KC)], axis=2),
        "params": params, "hist_b": history(i["state_conv_b"]), "hist_c": history(i["state_conv_c"]),
        "sub_keys": i["peer_sub_keys"].transpose(0, 4, 1, 2, 3).reshape(L, P, HP, P),
    }


_OUTS = {
    "y_out": (P, KC, T), "v_out": (DEPTH, NS, 512), "hb_p": (DEPTH, P, BC, WB - 1), "hb_s": (DEPTH, P, BC, NS, WB - 1),
    "hc_p": (DEPTH, P, BC, WC - 1), "hc_s": (DEPTH, P, BC, NS, WC - 1),
}


def kernel(**inputs):
    import numpy as np
    import concourse.bacc as bacc
    from concourse.bass_utils import run_bass_kernel_spmd

    arrays = {k: np.ascontiguousarray(v) for k, v in _lay_out({k: np.asarray(v) for k, v in inputs.items()}, np).items()}
    nc = bacc.Bacc("TRN2", target_bir_lowering=False, num_devices=1)
    args = {k: nc.dram_tensor(k, a.shape, mybir.dt.from_np(a.dtype), kind="ExternalInput").ap() for k, a in arrays.items()}
    args |= {k: nc.dram_tensor(k, s, F32, kind="ExternalOutput").ap() for k, s in _OUTS.items()}
    build(nc, **args)
    r = run_bass_kernel_spmd(nc, [arrays], core_ids=[0]).results[0]
    y = np.asarray(r["y_out"]).transpose(2, 1, 0).reshape(T, D)

    def rows(a):
        a = np.moveaxis(np.asarray(a), (2, 1), (-2, -1))
        return np.ascontiguousarray(a.reshape(*a.shape[:-2], -1))

    return (np.ascontiguousarray(y[:SEQ]).reshape(1, SEQ, D), np.ascontiguousarray(y[SEQ:]).reshape(NS, 1, D),
            np.asarray(r["v_out"]).reshape(DEPTH, NS, 1, 512), rows(r["hb_p"])[:, None], rows(r["hb_s"]),
            rows(r["hc_p"])[:, None], rows(r["hc_s"]))
```
